# Optimizing a Trainium2 kernel written in Bass

```python
import jax, jax.numpy as jnp
from jax import lax
import numpy as np

D_MODEL = 2048
BATCH = 1
SEQ = 256
DEPTH = 1

PLE_DIM = 256
CONV_DIM = 1024
CONV_K = 3
MLSTM_HEADS = 4
MLSTM_HEAD_DIM = 256
MLSTM_DIM = MLSTM_HEADS * MLSTM_HEAD_DIM
MLSTM_CHUNK = 128
MIX_DIM = CONV_DIM + MLSTM_DIM
IN_COLS = 3 * CONV_DIM + 4 * MLSTM_DIM + 2 * MLSTM_HEADS
PEER_HEADS = 8
PEER_N_KEYS = 128
PEER_N_EXPERTS = PEER_N_KEYS * PEER_N_KEYS
PEER_KEY_DIM = 256
PEER_HALF = PEER_KEY_DIM // 2
PEER_TOPK = 16
PEER_TOKEN_BLOCK = 128
EPS = 1e-6

kernel_name = "hybrid_conv_mlstm_peer_block"

def rmsnorm(x, g):
    xf = x.astype(jnp.float32)
    r = lax.rsqrt(jnp.mean(xf * xf, axis=-1, keepdims=True) + EPS)
    return (xf * r).astype(x.dtype) * g

def short_conv(b_gate, c_gate, u, w):
    z = c_gate * u
    s = z.shape[1]
    zp = jnp.pad(z, ((0, 0), (CONV_K - 1, 0), (0, 0)))
    y = w[0] * zp[:, 0:s]
    for j in range(1, CONV_K):
        y = y + w[j] * zp[:, j:j + s]
    return b_gate * y

def mlstm_chunkwise(q, k, v, i_pre, f_pre):
    bsz, s, nh, d = q.shape
    L = MLSTM_CHUNK
    nc = s // L

    def to_chunks(t):
        t = t.reshape((bsz, nc, L, nh) + t.shape[3:])
        return jnp.moveaxis(t, (1, 3), (0, 2))

    f32 = jnp.float32
    qc = to_chunks(q.astype(f32))
    kc = to_chunks(k.astype(f32)) * (d ** -0.5)
    vc = to_chunks(v.astype(f32))
    ic = to_chunks(i_pre.astype(f32))
    lfc = to_chunks(jax.nn.log_sigmoid(f_pre.astype(f32)))
    causal = jnp.tril(jnp.ones((L, L), dtype=bool))

    def step(carry, inp):
        C, n, m = carry
        qt, kt, vt, it, lft = inp
        b = jnp.cumsum(lft, axis=-1)
        dmat = jnp.where(causal, b[..., :, None] - b[..., None, :] + it[..., None, :], -jnp.inf)
        inter = b + m[..., None]
        m_t = jnp.maximum(inter, jnp.max(dmat, axis=-1))
        pw = jnp.exp(dmat - m_t[..., None])
        sc = jnp.einsum('bhtd,bhsd->bhts', qt, kt) * pw
        a = jnp.exp(inter - m_t)
        num = a[..., None] * jnp.einsum('bhtd,bhde->bhte', qt, C) + jnp.einsum('bhts,bhse->bhte', sc, vt)
        den = a * jnp.einsum('bhtd,bhd->bht', qt, n) + jnp.sum(sc, axis=-1)
        h = num / jnp.maximum(jnp.abs(den), jnp.exp(-m_t))[..., None]
        m_new = m_t[..., -1]
        w_s = jnp.exp(b[..., -1:] - b + it - m_new[..., None])
        a_l = jnp.exp(b[..., -1] + m - m_new)
        C_new = a_l[..., None, None] * C + jnp.einsum('bhs,bhsd,bhse->bhde', w_s, kt, vt)
        n_new = a_l[..., None] * n + jnp.einsum('bhs,bhsd->bhd', w_s, kt)
        return (C_new, n_new, m_new), h

    init = (jnp.zeros((bsz, nh, d, d), f32), jnp.zeros((bsz, nh, d), f32), jnp.zeros((bsz, nh), f32))
    _, hs = lax.scan(step, init, (qc, kc, vc, ic, lfc))
    return jnp.moveaxis(hs, (0, 2), (1, 3)).reshape(bsz, s, nh, d)

def peer(xn, wq, sub_keys, u_tab, v_tab):
    bsz, s, dm = xn.shape
    q = (xn @ wq).reshape(bsz, s, PEER_HEADS, 2, PEER_HALF)
    scores = jnp.einsum('bshpc,hpnc->bshpn', q, sub_keys).astype(jnp.float32)
    s_top, i_top = lax.top_k(scores, PEER_TOPK)
    cand_s = s_top[..., 0, :, None] + s_top[..., 1, None, :]
    cand_i = i_top[..., 0, :, None] * PEER_N_KEYS + i_top[..., 1, None, :]
    cand_s = cand_s.reshape(bsz, s, PEER_HEADS, PEER_TOPK * PEER_TOPK)
    cand_i = cand_i.reshape(bsz, s, PEER_HEADS, PEER_TOPK * PEER_TOPK)
    best_s, pos = lax.top_k(cand_s, PEER_TOPK)
    idx = jnp.take_along_axis(cand_i, pos, axis=-1)
    gate = jax.nn.softmax(best_s, axis=-1).astype(xn.dtype)
    nb = (bsz * s) // PEER_TOKEN_BLOCK
    xb = xn.reshape(nb, PEER_TOKEN_BLOCK, dm)
    ib = idx.reshape(nb, PEER_TOKEN_BLOCK, PEER_HEADS, PEER_TOPK)
    gb = gate.reshape(nb, PEER_TOKEN_BLOCK, PEER_HEADS, PEER_TOPK)

    def block(args):
        xt, it, gt = args
        u = u_tab[it]
        a = jnp.einsum('thkd,td->thk', u, xt)
        w = jax.nn.gelu(a, approximate=False) * gt
        return jnp.einsum('thk,thkd->td', w, v_tab[it])

    out = lax.map(block, (xb, ib, gb))
    return out.reshape(bsz, s, dm)

def setup_inputs(seed: int = 0) -> dict:
    key = jax.random.key(seed)
    ks = jax.random.split(key, 17)
    nrm = jax.random.normal
    f32 = jnp.float32
    x = nrm(ks[0], (BATCH, SEQ, D_MODEL), f32)
    p = nrm(ks[1], (DEPTH, BATCH, SEQ, PLE_DIM), f32)
    norm_mix_g = 1.0 + 0.02 * nrm(ks[2], (DEPTH, D_MODEL), f32)
    w_in = nrm(ks[3], (DEPTH, D_MODEL, IN_COLS), f32) * D_MODEL ** -0.5
    conv_w = nrm(ks[4], (DEPTH, CONV_K, CONV_DIM), f32) * CONV_K ** -0.5
    gate_base = jnp.concatenate([jnp.full((DEPTH, MLSTM_HEADS), -2.0, f32),
                                 jnp.broadcast_to(jnp.linspace(3.0, 6.0, MLSTM_HEADS, dtype=f32), (DEPTH, MLSTM_HEADS))], axis=-1)
    mlstm_gate_b = gate_base + 0.1 * nrm(ks[5], (DEPTH, 2 * MLSTM_HEADS), f32)
    mlstm_norm_g = 1.0 + 0.02 * nrm(ks[6], (DEPTH, MLSTM_DIM), f32)
    w_out = nrm(ks[7], (DEPTH, MIX_DIM, D_MODEL), f32) * MIX_DIM ** -0.5
    norm_ffn_g = 1.0 + 0.02 * nrm(ks[8], (DEPTH, D_MODEL), f32)
    peer_wq = nrm(ks[9], (DEPTH, D_MODEL, PEER_HEADS * PEER_KEY_DIM), f32) * D_MODEL ** -0.5
    peer_keys = nrm(ks[10], (DEPTH, PEER_HEADS, 2, PEER_N_KEYS, PEER_HALF), f32) * PEER_HALF ** -0.5
    peer_u = nrm(ks[11], (DEPTH, PEER_N_EXPERTS, D_MODEL), f32) * D_MODEL ** -0.5
    peer_v = nrm(ks[12], (DEPTH, PEER_N_EXPERTS, D_MODEL), f32) * D_MODEL ** -0.5
    norm_ple_g = 1.0 + 0.02 * nrm(ks[13], (DEPTH, D_MODEL), f32)
    ple_w_gate = nrm(ks[14], (DEPTH, D_MODEL, D_MODEL), f32) * D_MODEL ** -0.5
    ple_w_proj = nrm(ks[15], (DEPTH, PLE_DIM, D_MODEL), f32) * PLE_DIM ** -0.5
    norm_final_g = 1.0 + 0.02 * nrm(ks[16], (D_MODEL,), f32)
    return {"x": x, "p": p, "norm_mix_g": norm_mix_g, "w_in": w_in, "conv_w": conv_w,
            "mlstm_gate_b": mlstm_gate_b, "mlstm_norm_g": mlstm_norm_g, "w_out": w_out,
            "norm_ffn_g": norm_ffn_g, "peer_wq": peer_wq, "peer_keys": peer_keys,
            "peer_u": peer_u, "peer_v": peer_v, "norm_ple_g": norm_ple_g,
            "ple_w_gate": ple_w_gate, "ple_w_proj": ple_w_proj, "norm_final_g": norm_final_g}

def reference(x, p, norm_mix_g, w_in, conv_w, mlstm_gate_b, mlstm_norm_g, w_out,
              norm_ffn_g, peer_wq, peer_keys, peer_u, peer_v, norm_ple_g,
              ple_w_gate, ple_w_proj, norm_final_g):
    bsz, s, _ = x.shape
    c, m = CONV_DIM, MLSTM_DIM
    splits = [c, 2 * c, 3 * c, 3 * c + m, 3 * c + 2 * m, 3 * c + 3 * m, 3 * c + 4 * m]
    h = x
    for i in range(DEPTH):
        xn = rmsnorm(h, norm_mix_g[i])
        proj = xn @ w_in[i]
        bc, cc, uc, q, k, v, o, gates = jnp.split(proj, splits, axis=-1)
        y_conv = short_conv(bc, cc, uc, conv_w[i])
        gates = gates.astype(jnp.float32) + mlstm_gate_b[i].astype(jnp.float32)
        i_pre, f_pre = gates[..., :MLSTM_HEADS], gates[..., MLSTM_HEADS:]
        hd = (bsz, s, MLSTM_HEADS, MLSTM_HEAD_DIM)
        hm = mlstm_chunkwise(q.reshape(hd), k.reshape(hd), v.reshape(hd), i_pre, f_pre)
        hm = rmsnorm(hm, mlstm_norm_g[i].reshape(MLSTM_HEADS, MLSTM_HEAD_DIM).astype(jnp.float32))
        y_m = jax.nn.sigmoid(o) * hm.reshape(bsz, s, MLSTM_DIM).astype(x.dtype)
        h = h + jnp.concatenate([y_conv, y_m], axis=-1) @ w_out[i]
        h = h + peer(rmsnorm(h, norm_ffn_g[i]), peer_wq[i], peer_keys[i], peer_u[i], peer_v[i])
        g = jax.nn.sigmoid(rmsnorm(h, norm_ple_g[i]) @ ple_w_gate[i])
        h = h + g * (p[i] @ ple_w_proj[i])
    return rmsnorm(h, norm_final_g)


_drawn_inputs = setup_inputs


def setup_inputs(seed=0):
    import zlib

    import numpy as np

    out = dict(_drawn_inputs(seed))
    spreads = {}
    factors = {'mlstm_norm_g': 8.0,
     'norm_ffn_g': 8.0,
     'peer_wq': 7.313,
     'peer_keys': 7.284,
     'peer_u': 8.0,
     'peer_v': 7.266,
     'norm_ple_g': 8.0,
     'norm_final_g': 2.908}
    for name, (base, spread) in spreads.items():
        noise = np.random.default_rng([zlib.crc32(name.encode()), seed]).standard_normal(out[name].shape)
        drawn = base * np.exp(spread * noise) if base else spread * noise
        out[name] = __import__('jax').numpy.asarray(drawn.astype(out[name].dtype))
    for name, factor in factors.items():
        out[name] = (out[name] * factor).astype(out[name].dtype)
    return out
```

```python
from contextlib import ExitStack

import concourse.bass as bass
from concourse import mybir

F32 = mybir.dt.float32
F32R = mybir.dt.float32r
U32 = mybir.dt.uint32
ALU = mybir.AluOpType
ACT = mybir.ActivationFunctionType
AX = mybir.AxisListType

P = 128
D = 2048
S = 256
TT = S // P
KT = D // P
KQ = KT // 4
NB = 512
ROUND = 2 * NB
CONV = 1024
TAPS = 3
H, HD = 4, 256
HW = HD + 1
CT = CONV // P
PH, TOPK, NK = 8, 16, 128
CAND = TOPK * TOPK
SLOTS = PH * TOPK
PLE = 256
PT = PLE // P
EPS = 1e-6
FAR = -3.0e38
G = 4
GROUPS = SLOTS // G
RING = 4
KH = KQ // 2
HALVES = 2
SPLIT = 4
EARLY = 6
UNITS = TT * PH - EARLY
UNIT_STEPS = 29
Q_AT, B_AT, GATES_AT = 3072, 0, 7168
BLOCKS_OUT, BLOCKS_WQ, BLOCKS_PLE = 4, 4, 4


class Count:

    def __init__(self, engine, sem):
        self.engine, self.sem, self.n, self.steps = engine, sem, 0, 0

    def done(self, instruction):
        instruction.then_inc(self.sem, 1)
        self.n, self.steps = self.n + 1, self.steps + 1

    def wait(self):
        self.engine.wait_ge(self.sem, self.n)

    def wait_apart(self, passed):
        self.wait()
        self.engine.sem_inc(passed, 1)


def build(nc, x, p, g_mix, w_in, conv_w, gate_b, g_mlstm, w_out, g_ffn, wq, keys, u_tab, v_tab,
          g_ple, w_gate, w_proj, g_final, out):
    ctx = ExitStack()
    with ctx:
        def sb(name, shape, dt=F32):
            return ctx.enter_context(nc.sbuf_tensor(name, shape, dt))

        def sem(name):
            return ctx.enter_context(nc.semaphore(name))

        w_hi = [sb(f"w_hi{i}", [P, KH, NB], F32R) for i in range(SPLIT)]
        w_lo = [sb(f"w_lo{i}", [P, KH, NB], F32R) for i in range(SPLIT)]
        h = sb("h", [P, TT, D])
        xn = sb("xn", [P, TT, D])
        xT_hi = sb("xT_hi", [P, KT, S], F32R)
        xT_lo = sb("xT_lo", [P, KT, S], F32R)
        pT = sb("pT", [P, PT, S])
        big = sb("big", [P, 2 * G * D + 24])

        at = [0]

        def view(size, pattern, **sizes):
            v = big[:, at[0]:at[0] + size].rearrange(pattern, **sizes)
            at[0] += size
            return v

        bT = view(CT * S, "p (c t) -> p c t", t=S)
        zT = view(CT * S, "p (c t) -> p c t", t=S)
        at[0] += 4 * H * HW - 2 * CT * S
        qT = view(CT * S, "p (c t) -> p c t", t=S)
        kT = view(CT * S, "p (c t) -> p c t", t=S)
        vS = view(TT * H * HW, "p (a h e) -> p a h e", a=TT, h=H)
        keysT = view(2 * PH * NK, "p (a n) -> p a n", n=NK)
        raw = [sb(f"raw{i}", [P, KQ, NB])[:, :, :] for i in range(2)] + \
            [view(KQ * NB, "p (k n) -> p k n", k=KQ) for i in range(2)]
        conv = qT
        o_sig = xn[:, 0, :].rearrange("p (a n) -> p a n", a=TT)
        state = big[:, 0:2 * H * HW].rearrange("p (h d e) -> p h d e", h=H, d=2)
        num = big[:, 2 * H * HW:4 * H * HW].rearrange("p (a h e) -> p a h e", a=TT, h=H)
        keys_raw = qT.rearrange("p c t -> p (c t)").rearrange("p (a c) -> p a c", c=P)
        p_raw = big[:, CT * S:CT * S + TT * PLE].rearrange("p (a c) -> p a c", a=TT)
        u_rows = [big[:, i * D:(i + 1) * D] for i in range(G)]
        v_rows = [big[:, (G + i) * D:(G + i + 1) * D] for i in range(G)]
        g_rows = u_rows[0]
        fin_rows = u_rows[1]
        wp = big[:, 2 * D:2 * D + PT * D].rearrange("p (k n) -> p k n", k=PT)
        q_heads = [v_rows[0][:, i * 4 * S:(i + 1) * 4 * S].rearrange("p (c t) -> p c t", t=S)
                   for i in range(2)]
        sig = [[v_rows[0][:, (2 * b + t) * NB:(2 * b + t + 1) * NB] for t in range(TT)] for b in range(2)]

        scores0 = sb("scores0", [P, 2, 4, NK])
        scores1 = sb("scores1", [P, 2 * UNITS, NK])
        scores_now = sb("scores_now", [P, 2, NK])
        tmp = sb("tmp", [P, 1024])
        pw = scores0[:, :, :, :].rearrange("p a h s -> p (a h) s")
        diag_e = scores1[:, 0:TT * H, :]
        scT = diag_e
        o_gain = scores1[:, TT * H:2 * TT * H, :].rearrange("p a n -> p (a n)")
        kN = tmp[:, :].rearrange("p (h d) -> p h d", h=H)
        v_diag = [tmp[:, i * P:(i + 1) * P] for i in range(G)]
        below_top = tmp[:, 512:512 + UNITS * TOPK]

        ident = sb("ident", [P, P])
        tri = sb("tri", [P, P])
        last_row = sb("last_row", [P, P])
        mask = sb("mask", [P, P])
        ones = sb("ones", [P, P])
        stack = sb("stack", [TAPS * CT, P])
        cols = sb("cols", [P, TAPS, CT])
        gw = sb("gw", [P, KT, 2 * H])
        gw_hi = sb("gw_hi", [P, KT, 2 * H], F32R)
        gw_lo = sb("gw_lo", [P, KT, 2 * H], F32R)
        gb = sb("gb", [P, 2 * H])
        eps = sb("eps", [P, 1])
        sq_sum = sb("sq_sum", [P, TT])
        root = sb("root", [P, TT])
        rstd = sb("rstd", [P, TT])
        gates = sb("gates", [P, TT, 2 * H])
        abs_f = sb("abs_f", [P, TT, H])
        exp_f = sb("exp_f", [P, TT, H])
        log_f = sb("log_f", [P, TT, H])
        lf = sb("lf", [P, TT, H])
        bcum = sb("bcum", [P, TT, H])
        e_in = sb("e_in", [P, TT, H])
        m_in = sb("m_in", [P, TT, H])
        m_t = sb("m_t", [P, TT, H])
        neg_m = sb("neg_m", [P, TT, H])
        mb = sb("mb", [P, 2 * H])
        mb_last = sb("mb_last", [P, 2 * H])
        inter = sb("inter", [P, H])
        decay = sb("decay", [P, 2, H])
        floor = sb("floor", [P, TT, H])
        den = sb("den", [P, TT, H])
        rden = sb("rden", [P, TT, H])
        head_sq = sb("head_sq", [P, TT, H])
        head_root = sb("head_root", [P, TT, H])
        head_scale = sb("head_scale", [P, TT, H])

        iota16 = sb("iota16", [P, TOPK])
        top_s = sb("top_s", [P, 2, 2, TOPK])
        top_i = sb("top_i", [P, 2, 2, TOPK], U32)
        top_f = sb("top_f", [P, 2, 2, TOPK])
        best = sb("best", [P, 2, TOPK])
        pos = sb("pos", [P, 2, TOPK], U32)
        pos_a = sb("pos_a", [P, 2, TOPK], U32)
        pos_b = sb("pos_b", [P, 2, TOPK], U32)
        pos_f = [sb(f"pos_f{i}", [P, 2, TOPK]) for i in range(2)]
        sel = [sb(f"sel{i}", [P, 2, TOPK]) for i in range(2)]
        expert = sb("expert", [P, TT * SLOTS + G], U32)
        gate = sb("gate", [P, TT * SLOTS])
        gate_sum = sb("gate_sum", [P, TT * PH])
        gate_inv = sb("gate_inv", [P, TT * PH])
        idx_now = [sb(f"idx_now{i}", [P, G], U32) for i in range(2)]
        gate_now = [sb(f"gate_now{i}", [P, G]) for i in range(2)]
        dots = [sb(f"dots{i}", [P, G]) for i in range(2)]
        act_now = [sb(f"act_now{i}", [P, G]) for i in range(2)]

        ps = [ctx.enter_context(nc.psum_tensor(f"ps{i}", [P, NB], F32)) for i in range(8)]

        x_in = [sem(f"x_in{t}") for t in range(TT)]
        small_in = [sem(f"small_in{i}") for i in range(6)]
        gain_in = [sem(f"gain_in{i}") for i in range(3)]
        final_in = sem("final_in")
        wp_in = sem("wp_in")
        raw_in = [sem(f"raw_in{i}") for i in range(RING)]
        hi_ready = sem("hi_ready")
        lo_ready = sem("lo_ready")
        half_used = sem("half_used")
        consts = sem("consts")
        free_v = sem("free_v")
        sq_done = sem("sq_done")
        xn_ready = sem("xn_ready")
        tr_mm = sem("tr_mm")
        xT_a = sem("xT_a")
        xT_v = sem("xT_v")
        gw_a = sem("gw_a")
        gw_v = sem("gw_v")
        setup_mm = sem("setup_mm")
        setup_v = sem("setup_v")
        abs_ready = sem("abs_ready")
        softplus = sem("softplus")
        lf_ready = sem("lf_ready")
        diag_e_ready = sem("diag_e_ready")
        mix_mm = sem("mix_mm")
        mb_ready = sem("mb_ready")
        m_ready = sem("m_ready")
        pw_ready = sem("pw_ready")
        sc_ready = sem("sc_ready")
        kN_ready = sem("kN_ready")
        scT_ready = sem("scT_ready")
        bank_mm = sem("bank_mm")
        bank_a = sem("bank_a")
        bank_v = sem("bank_v")
        o_out = sem("o_out")
        rden_ready = sem("rden_ready")
        head_rt = sem("head_rt")
        y_ready = sem("y_ready")
        yT_mm = sem("yT_mm")
        yT_a = sem("yT_a")
        yT_v = sem("yT_v")
        conv_ready = sem("conv_ready")
        conv_a = sem("conv_a")
        conv_v = sem("conv_v")
        q_out = sem("q_out")
        scores_mm = sem("scores_mm")
        scores_out = sem("scores_out")
        scores_used = sem("scores_used")
        now_ready = sem("now_ready")
        now_used = sem("now_used")
        below_ready = sem("below_ready")
        gate_exp = sem("gate_exp")
        idx_ready = sem("idx_ready")
        gate_c = sem("gate_c")
        u_in = [sem(f"u_in{i}") for i in range(G)]
        v_in = [sem(f"v_in{i}") for i in range(G)]
        u_used = sem("u_used")
        v_used = sem("v_used")
        act_ready = sem("act_ready")
        diag_ready = sem("diag_ready")
        peer_out = sem("peer_out")
        ple_mm = sem("ple_mm")
        sig_out = sem("sig_out")
        ple_used = sem("ple_used")
        ple_added = sem("ple_added")
        out_ready = sem("out_ready")
        stored = [sem(f"stored{t}") for t in range(TT)]
        act_c = sem("act_c")
        dve_c = sem("dve_c")
        pool_c = sem("pool_c")
        passed_v, passed_p, passed_s = sem("passed_v"), sem("passed_p"), sem("passed_s")

        OUT0, WQ0, PLE0 = 14, 18, 22
        ORDER_IN, ORDER_OUT = (0, 1, 2, 3), (2, 3, 0, 1)

        def through(n):
            return SPLIT + HALVES * RING * (n + 1)

        block = ctx.enter_context(nc.Block())

        @block.sync
        def _(sp):
            for t in range(TT):
                sp.dma_start(h[:, t, :], x[t * P:(t + 1) * P, :]).then_inc(x_in[t], 16)
            sp.dma_start(g_rows, g_mix.to_broadcast([P, D])).then_inc(gain_in[0], 16)

            def load(slot, n, src, quarter, col):
                sp.wait_ge(lo_ready, n * HALVES + HALVES)
                sp.sem_inc(passed_s, 1)
                sp.dma_start(raw[slot], src.rearrange("(k p) n -> p k n", p=P)
                             [:, quarter * KQ:(quarter + 1) * KQ, bass.ds(col, NB)]).then_inc(raw_in[slot], 16)

            def stream(src, at, blocks, block0, order=ORDER_IN):
                with sp.Fori(0, blocks) as i:
                    for j, quarter in enumerate(order):
                        load(j, i * RING + (block0 * RING + j), src, quarter, i * NB + at)

            stream(w_in, Q_AT, 8, 0)
            stream(w_in, B_AT, 6, 8)
            stream(w_out, 0, BLOCKS_OUT, OUT0, ORDER_OUT)
            sp.wait_ge(conv_v, 2)
            sp.dma_start(g_rows, g_ffn.to_broadcast([P, D])).then_inc(gain_in[1], 16)
            stream(wq, 0, BLOCKS_WQ, WQ0)
            for j in range(2):
                load(j, PLE0 * RING + j, w_gate, j, 0)
            sp.wait_ge(u_used, G + TT * SLOTS)
            sp.dma_start(g_rows, g_ple.to_broadcast([P, D])).then_inc(gain_in[2], 16)
            sp.dma_start(wp, w_proj.rearrange("(k p) n -> p k n", p=P)).then_inc(wp_in, 16)
            sp.wait_ge(v_used, G + TT * SLOTS)
            for j in range(2, RING):
                load(j, PLE0 * RING + j, w_gate, j, 0)
            sp.dma_start(fin_rows, g_final.to_broadcast([P, D])).then_inc(final_in, 16)
            stream(w_gate, NB, BLOCKS_PLE - 1, PLE0 + 1)
            for t in range(TT):
                sp.wait_ge(out_ready, t + 1)
                sp.dma_start(out[t * P:(t + 1) * P, :], xn[:, t, :]).then_inc(stored[t], 16)
            for t in range(TT):
                sp.wait_ge(stored[t], 16)

        @block.gpsimd
        def _(pool):
            step = Count(pool, pool_c)
            step.done(pool.memset(ident[:, :], 0.0))
            step.done(pool.memset(ones[:, :], 1.0))
            step.done(pool.memset(mask[:, :], 0.0))
            step.done(pool.memset(eps[:, :], EPS))
            step.done(pool.memset(vS[:, :, :, HD:HW], 1.0))
            step.done(pool.memset(expert[:, TT * SLOTS:TT * SLOTS + G], 0))
            step.wait()
            pool.affine_select(out=ident[:, :], in_=ident[:, :], compare_op=ALU.not_equal, fill=1.0,
                               base=0, pattern=[[-1, P]], channel_multiplier=1).then_inc(consts, 1)
            pool.affine_select(out=tri[:, :], in_=ones[:, :], compare_op=ALU.is_ge, fill=0.0,
                               base=0, pattern=[[1, P]], channel_multiplier=-1).then_inc(consts, 1)
            pool.affine_select(out=mask[:, :], in_=mask[:, :], compare_op=ALU.is_ge, fill=FAR,
                               base=0, pattern=[[-1, P]], channel_multiplier=1).then_inc(consts, 1)
            pool.affine_select(out=last_row[:, :], in_=ones[:, :], compare_op=ALU.is_ge, fill=0.0,
                               base=-(P - 1), pattern=[[0, P]], channel_multiplier=1).then_inc(consts, 1)
            pool.iota(iota16[:, :], pattern=[[1, TOPK]], base=0, channel_multiplier=0,
                      allow_small_or_imprecise_dtypes=True).then_inc(consts, 1)

            def make_lo(n, slot):
                for part in range(HALVES):
                    buffer = (HALVES * slot + part) % SPLIT
                    pool.wait_ge(hi_ready, n * HALVES + (part + 1))
                    pool.tensor_tensor(w_lo[buffer][:, :, :], raw[slot][:, part * KH:(part + 1) * KH, :],
                                       w_hi[buffer][:, :, :].bitcast(F32), ALU.subtract).then_inc(lo_ready, 1)

            with pool.Fori(0, PLE0) as i:
                for j in range(RING):
                    make_lo(i * RING + j, j)
            for j in range(2):
                make_lo(PLE0 * RING + j, j)
            pool.wait_ge(lo_ready, HALVES * RING * (PLE0 + 1))

            for t in range(TT):
                with pool.Fori(0, GROUPS // 2) as i:
                    for par in range(2):
                        g = i * 2 + (t * GROUPS + par)
                        pool.wait_ge(idx_ready, g + 1)
                        pool.wait_ge(u_used, g * G + G)
                        pool.sem_inc(passed_p, 1)
                        for s in range(G):
                            pool.indirect_dma_start(
                                out=u_rows[s], out_offset=None, in_=u_tab[:, :],
                                in_offset=bass.IndirectOffsetOnAxis(ap=idx_now[par][:, s:s + 1], axis=0),
                            ).then_inc(u_in[s], 16)
                        for s in range(G):
                            pool.wait_ge(v_used, g * G + (s + 1))
                            pool.sem_inc(passed_p, 1)
                            pool.indirect_dma_start(
                                out=v_rows[s], out_offset=None, in_=v_tab[:, :],
                                in_offset=bass.IndirectOffsetOnAxis(ap=idx_now[par][:, s:s + 1], axis=0),
                            ).then_inc(v_in[s], 16)

            for j in range(2, RING):
                make_lo(PLE0 * RING + j, j)
            with pool.Fori(PLE0 + 1, PLE0 + BLOCKS_PLE) as i:
                for j in range(RING):
                    make_lo(i * RING + j, j)

        @block.tensor
        def _(pe):
            pe.sem_inc(lo_ready, HALVES * RING)
            pe.sem_inc(half_used, SPLIT)
            pe.sem_inc(free_v, 4)
            pe.sem_inc(scores_out, 2)
            pe.sem_inc(sig_out, 4)
            pe.sem_inc(ple_used, 4)
            pe.sem_inc(u_used, G)
            pe.sem_inc(now_used, 1)
            pe.wait_ge(consts, 5)

            def transpose_norm(norm):
                for s in range(8):
                    t, q = s // 4, s % 4
                    if q == 0:
                        pe.wait_ge(xn_ready, norm * TT + t + 1)
                    if s >= 4:
                        pe.wait_ge(xT_v, norm * 8 + s - 3)
                    for j in range(4):
                        last = nc.tensor.transpose(ps[4 + q][:, j * P:(j + 1) * P],
                                                   xn[:, t, (4 * q + j) * P:(4 * q + j + 1) * P], ident[:, :])
                    last.then_inc(tr_mm, 1)
                pe.wait_ge(xT_v, norm * 8 + 8)

            def wait_half(i, block0, half):
                pe.wait_ge(lo_ready, i * (HALVES * RING) + (HALVES * RING * (block0 + 1) + half + 1))

            def channel_block(b, i, block0, halves=(0, HALVES * RING)):
                for j in range(*halves):
                    wait_half(i, block0, j)
                    hi, lo = w_hi[j % SPLIT], w_lo[j % SPLIT]
                    for c in range(4):
                        out_c = ps[2 * b + c // 2][:, c % 2 * S:(c % 2 + 1) * S]
                        for k in range(KH):
                            kk = j * KH + k
                            nc.tensor.matmul(out_c, lo[:, k, c * P:(c + 1) * P], xT_hi[:, kk, :],
                                             start=(kk == 0 and c % 2 == 0), stop=False)
                            nc.tensor.matmul(out_c, hi[:, k, c * P:(c + 1) * P], xT_lo[:, kk, :],
                                             start=False, stop=False)
                            last = nc.tensor.matmul(out_c, hi[:, k, c * P:(c + 1) * P], xT_hi[:, kk, :],
                                                    start=False, stop=(kk == KT - 1 and c % 2 == 1))
                    last.then_inc(half_used, 1)

            def token_block(b, i, block0, order=ORDER_IN):
                for j in range(HALVES * RING):
                    quarter = order[j // HALVES]
                    wait_half(i, block0, j)
                    if order == ORDER_OUT and quarter == 0 and j % HALVES == 0:
                        pe.wait_ge(conv_v, 2)
                    hi, lo = w_hi[j % SPLIT], w_lo[j % SPLIT]
                    for t in range(TT):
                        for k in range(KH):
                            kk = quarter * KQ + j % HALVES * KH + k
                            nc.tensor.matmul(ps[2 * b + t][:, :], xT_lo[:, kk, t * P:(t + 1) * P], hi[:, k, :],
                                             start=(j == 0 and k == 0), stop=False)
                            nc.tensor.matmul(ps[2 * b + t][:, :], xT_hi[:, kk, t * P:(t + 1) * P], lo[:, k, :],
                                             start=False, stop=False)
                            last = nc.tensor.matmul(ps[2 * b + t][:, :], xT_hi[:, kk, t * P:(t + 1) * P], hi[:, k, :],
                                                    start=False, stop=(j == HALVES * RING - 1 and k == KH - 1))
                    last.then_inc(half_used, 1)

            transpose_norm(0)

            pe.wait_ge(gw_v, 1)
            for t in range(TT):
                for k in range(KT):
                    gates_t = ps[4][:, t * 8:(t + 1) * 8]
                    nc.tensor.matmul(gates_t, xT_lo[:, k, t * P:(t + 1) * P], gw_hi[:, k, :],
                                     start=(k == 0 and t == 0), stop=False)
                    nc.tensor.matmul(gates_t, xT_hi[:, k, t * P:(t + 1) * P], gw_lo[:, k, :], start=False, stop=False)
                    last = nc.tensor.matmul(gates_t, xT_hi[:, k, t * P:(t + 1) * P], gw_hi[:, k, :],
                                            start=False, stop=(k == KT - 1 and t == 1))
            last.then_inc(setup_mm, 1)
            pe.wait_ge(small_in[2], 16)
            rows = TAPS * CT
            nc.tensor.transpose(ps[5][:, 0:rows], stack[:, :], ident[0:rows, 0:rows]).then_inc(setup_mm, 1)
            pe.wait_ge(small_in[4], 16)
            for t in range(TT):
                for k in range(PT):
                    last = nc.tensor.transpose(ps[6][:, k * S + t * P:k * S + (t + 1) * P],
                                               p_raw[:, t, k * P:(k + 1) * P], ident[:, :])
            last.then_inc(setup_mm, 1)
            pe.wait_ge(small_in[5], 16)
            for n, bank in enumerate((7, 5, 6, 7)):
                if n:
                    pe.wait_ge(setup_v, n)
                for j in range(4):
                    last = nc.tensor.transpose(ps[bank][:, j * P:(j + 1) * P], keys_raw[:, 4 * n + j, :], ident[:, :])
                last.then_inc(setup_mm, 1)
            pe.wait_ge(lf_ready, 1)
            nc.tensor.matmul(ps[4][:, 256:264], tri[:, :], lf[:, :, :].rearrange("p a h -> p (a h)"),
                             start=True, stop=True).then_inc(setup_mm, 1)

            with pe.Fori(0, 2) as i:
                for b in range(2):
                    pe.wait_ge(free_v, i * 4 + (2 * b + 2))
                    channel_block(b, i * 2, b)

            pe.wait_ge(diag_e_ready, 1)
            pe.wait_ge(setup_v, 6)
            for a in range(TT):
                last = nc.tensor.matmul(ps[4 + a][:, :], ones[:, :],
                                        diag_e[:, a * H:(a + 1) * H, :].rearrange("p h s -> p (h s)"),
                                        start=True, stop=True)
            last.then_inc(mix_mm, 1)
            pe.wait_ge(free_v, 4 + 8)
            for a in range(TT):
                for hh in range(H):
                    for d in range(2):
                        last = nc.tensor.matmul(
                            ps[6 + a][:, hh * P:(hh + 1) * P], qT[:, 2 * hh + d, a * P:(a + 1) * P],
                            kT[:, 2 * hh + d, a * P:(a + 1) * P], start=(hh == 0 and d == 0),
                            stop=(hh == H - 1 and d == 1))
            last.then_inc(mix_mm, 1)
            pe.wait_ge(mb_ready, 1)
            nc.tensor.matmul(ps[4][:, 0:2 * H], last_row[:, :], mb[:, :], start=True, stop=True).then_inc(mix_mm, 1)

            with pe.Fori(0, 2) as i:
                for b in range(2):
                    pe.wait_ge(free_v, i * 4 + (2 * b + 10))
                    token_block(b, i * 2, 4 + b)

            pe.wait_ge(m_ready, 1)
            for c in range(CT):
                last = nc.tensor.transpose(ps[4 + c // 4][:, c % 4 * P:(c % 4 + 1) * P], kT[:, c, 0:P], ident[:, :])
            last.then_inc(mix_mm, 1)
            pe.wait_ge(sc_ready, 1)
            for c in range(TT * H):
                last = nc.tensor.transpose(ps[6 + c // H][:, c % H * P:(c % H + 1) * P], pw[:, c, :], ident[:, :])
            last.then_inc(mix_mm, 1)

            pe.wait_ge(scT_ready, 1)
            pe.wait_ge(free_v, 4 + 16)
            for hh in range(H):
                nc.tensor.matmul(ps[hh][:, 0:HW], scT[:, hh, :], vS[:, 0, hh, :], start=True, stop=True)\
                    .then_inc(bank_mm, 1)
            pe.wait_ge(kN_ready, 1)
            for n in range(2 * H):
                if n >= 4:
                    pe.wait_ge(bank_a, n - 3)
                nc.tensor.matmul(ps[(4 + n) % 8][:, 0:HW], kN[:, n // 2, n % 2 * P:(n % 2 + 1) * P],
                                 vS[:, 0, n // 2, :], start=True, stop=True).then_inc(bank_mm, 1)
            for hh in range(H):
                if hh % 2 == 0:
                    pe.wait_ge(bank_a, 4 + hh // 2 + 1)
                else:
                    pe.wait_ge(bank_v, hh // 2 + 1)
                nc.tensor.matmul(ps[4 + hh][:, 0:HW], scT[:, H + hh, :], vS[:, 1, hh, :], start=True, stop=True)\
                    .then_inc(bank_mm, 1)
            pe.wait_ge(bank_a, 8)
            pe.wait_ge(bank_v, 4)
            for hh in range(H):
                for d in range(2):
                    last = nc.tensor.matmul(ps[hh][:, 0:HW], qT[:, 2 * hh + d, P:2 * P], state[:, hh, d, :],
                                            start=(d == 0), stop=(d == 1))
                last.then_inc(bank_mm, 1)

            pe.wait_ge(bank_v, 8)
            with pe.Fori(0, 3) as i:
                for b in range(2):
                    pe.wait_ge(free_v, i * 4 + (2 * b + 18))
                    channel_block(b, i * 2, 8 + b)

            pe.wait_ge(y_ready, 1)
            for s in range(4):
                for j in range(4):
                    c = s % 2 * 4 + j
                    last = nc.tensor.transpose(ps[4 + s][:, j * P:(j + 1) * P],
                                               o_sig[:, s // 2, c * P:(c + 1) * P], ident[:, :])
                last.then_inc(yT_mm, 1)
            pe.wait_ge(yT_v, 4)

            with pe.Fori(0, 2) as i:
                for b in range(2):
                    pe.wait_ge(free_v, i * 4 + (2 * b + 30))
                    token_block(b, i * 2, OUT0 + b, ORDER_OUT)

            transpose_norm(1)

            def scores(b, i):
                pe.wait_ge(q_out, i * 4 + (2 * b + 2))
                pe.wait_ge(scores_out, i * 2 + (b + 1))
                for t in range(TT):
                    for c in range(4):
                        last = nc.tensor.matmul(
                            ps[4 + 2 * b + t][:, c * P:(c + 1) * P], q_heads[b][:, c, t * P:(t + 1) * P],
                            keysT[:, bass.ds(i * 8 + (4 * b + c), 1), :].rearrange("p a n -> p (a n)"),
                            start=(c == 0), stop=(c == 3))
                last.then_inc(scores_mm, 1)

            with pe.Fori(0, 2) as i:
                channel_block(0, i * 2, WQ0)
                channel_block(1, i * 2, WQ0 + 1, (0, HALVES))
                scores(0, i)
                channel_block(1, i * 2, WQ0 + 1, (HALVES, HALVES * RING))
                scores(1, i)
            pe.wait_ge(scores_mm, BLOCKS_WQ)
            pe.sem_inc(v_used, G)

            pe.wait_ge(scores_out, 6)
            for t in range(TT):
                for n in range(4):
                    nc.tensor.matmul(ps[4 * t + n][:, :], ident[:, :], h[:, t, n * NB:(n + 1) * NB],
                                     start=True, stop=True)
                with pe.Fori(0, GROUPS // 2) as i:
                    for par in range(2):
                        g = i * 2 + (t * GROUPS + par)
                        for s in range(G):
                            pe.wait_ge(v_in[s], g * 16 + 16)
                            pe.wait_ge(diag_ready, g * G + (s + 1))
                            for n in range(4):
                                last = nc.tensor.matmul(ps[4 * t + n][:, :], v_diag[s],
                                                        v_rows[s][:, n * NB:(n + 1) * NB],
                                                        start=False, stop=True, skip_group_check=True)
                            last.then_inc(v_used, 1)

            transpose_norm(2)

            with pe.Fori(0, 2) as i:
                for b in range(2):
                    pe.wait_ge(sig_out, i * 4 + (2 * b + 2))
                    token_block(b, i * 2, PLE0 + b)
                    pe.wait_ge(ple_used, i * 4 + (2 * b + 2))
                    pe.wait_ge(wp_in, 16)
                    for t in range(TT):
                        for k in range(PT):
                            last = nc.tensor.matmul(ps[4 + 2 * b + t][:, :], pT[:, k, t * P:(t + 1) * P],
                                                    wp[:, k, bass.ds(i * ROUND + b * NB, NB)],
                                                    start=(k == 0), stop=(k == PT - 1))
                    last.then_inc(ple_mm, 1)

        @block.scalar
        def _(act):
            step = Count(act, act_c)
            act.dma_start(gw[:, :, :], w_in[:, GATES_AT:GATES_AT + 2 * H].rearrange("(k p) n -> p k n", p=P))\
                .then_inc(small_in[0], 16)
            act.dma_start(gb[:, :], gate_b.to_broadcast([P, 2 * H])).then_inc(small_in[1], 16)
            act.dma_start(stack[:, :], conv_w.rearrange("j (c p) -> (j c) p", p=P)).then_inc(small_in[2], 16)
            act.dma_start(o_gain, g_mlstm.to_broadcast([P, CONV])).then_inc(small_in[3], 16)
            act.dma_start(p_raw, p.rearrange("(a t) c -> t a c", t=P)).then_inc(small_in[4], 16)
            act.dma_start(keys_raw, keys.rearrange("a n c -> n a c")).then_inc(small_in[5], 16)
            act.wait_ge(pool_c, 6)

            def mean_square(t):
                step.done(nc.scalar.activation(xn[:, t, :], h[:, t, :], ACT.Square, accum_out=sq_sum[:, t:t + 1]))
                step.wait()
                nc.scalar.activation(root[:, t:t + 1], sq_sum[:, t:t + 1], ACT.Sqrt, bias=eps[:, :],
                                     scale=1.0 / D).then_inc(sq_done, 1)

            def transposes_hi(norm):
                for s in range(8):
                    act.wait_ge(tr_mm, norm * 8 + s + 1)
                    nc.scalar.activation(xT_hi[:, s % 4 * 4:s % 4 * 4 + 4, s // 4 * P:(s // 4 + 1) * P],
                                         ps[4 + s % 4][:, :].rearrange("p (k t) -> p k t", k=4), ACT.Copy)\
                        .then_inc(xT_a, 1)

            def make_hi(turn, n, slot):
                act.wait_ge(raw_in[slot], turn * 16 + 16)
                for part in range(HALVES):
                    act.wait_ge(half_used, n * HALVES + (part + 1))
                    nc.scalar.activation(w_hi[(HALVES * slot + part) % SPLIT][:, :, :],
                                         raw[slot][:, part * KH:(part + 1) * KH, :], ACT.Copy).then_inc(hi_ready, 1)

            def hi_quarters(first, last):
                for n in range(first, last):
                    make_hi(n // RING, n, n % RING)

            def hi_blocks(first, last):
                with act.Fori(first, last) as i:
                    for j in range(RING):
                        make_hi(i, i * RING + j, j)

            for t in range(TT):
                act.wait_ge(x_in[t], 16)
                mean_square(t)
            act.wait_ge(small_in[0], 16)
            nc.scalar.activation(gw_hi[:, :, :], gw[:, :, :], ACT.Copy).then_inc(gw_a, 1)
            transposes_hi(0)
            hi_quarters(0, 2)

            act.wait_ge(abs_ready, 1)
            step.done(nc.scalar.activation(exp_f[:, :, :], abs_f[:, :, :], ACT.Exp, scale=-1.0))
            step.wait()
            nc.scalar.activation(log_f[:, :, :], exp_f[:, :, :], ACT.Ln, bias=1.0).then_inc(softplus, 1)

            hi_quarters(2, RING)
            hi_blocks(1, 5)

            act.wait_ge(m_ready, 1)
            for a in range(TT):
                for hh in range(H):
                    nc.scalar.activation(pw[:, a * H + hh, :], pw[:, a * H + hh, :], ACT.Exp,
                                         bias=neg_m[:, a, hh:hh + 1])
            nc.scalar.activation(decay[:, :, :], decay[:, :, :], ACT.Exp)
            nc.scalar.activation(floor[:, :, :], neg_m[:, :, :], ACT.Exp).then_inc(pw_ready, 1)

            hi_blocks(5, 8)
            hi_quarters(8 * RING, 8 * RING + 2)

            act.wait_ge(free_v, 4 + 16)
            nc.scalar.activation(o_sig, o_sig, ACT.Sigmoid).then_inc(o_out, 1)
            for hh in range(H):
                act.wait_ge(bank_mm, hh + 1)
                nc.scalar.activation(num[:, 0, hh, :], ps[hh][:, 0:HW], ACT.Copy).then_inc(bank_a, 1)
            for hh in range(H):
                act.wait_ge(bank_mm, 4 + 2 * hh + 1)
                nc.scalar.activation(state[:, hh, 0, :], ps[(4 + 2 * hh) % 8][:, 0:HW], ACT.Copy).then_inc(bank_a, 1)
            for hh in range(H):
                act.wait_ge(bank_mm, 12 + hh + 1)
                nc.scalar.activation(num[:, 1, hh, :], ps[4 + hh][:, 0:HW], ACT.Copy).then_inc(bank_a, 1)

            act.wait_ge(rden_ready, 1)
            for a in range(TT):
                for hh in range(H):
                    step.done(nc.scalar.activation(ps[4 + hh][:, 0:HD], num[:, a, hh, 0:HD], ACT.Square,
                                                   scale=rden[:, a, hh:hh + 1], accum_out=head_sq[:, a, hh:hh + 1]))
                step.wait()
            nc.scalar.activation(head_root[:, :, :], head_sq[:, :, :], ACT.Sqrt, bias=eps[:, :], scale=1.0 / HD)\
                .then_inc(head_rt, 1)

            hi_quarters(8 * RING + 2, 9 * RING)
            hi_blocks(9, 13)
            hi_quarters(13 * RING, 14 * RING)
            act.wait_ge(conv_ready, 1)
            nc.scalar.activation(xT_hi[:, 0:4, :], conv[:, 0:4, :], ACT.Copy).then_inc(conv_a, 1)
            hi_quarters(14 * RING, 14 * RING + 2)
            for s in range(4):
                act.wait_ge(yT_mm, s + 1)
                c = CT + s % 2 * 4
                nc.scalar.activation(xT_hi[:, c:c + 4, s // 2 * P:(s // 2 + 1) * P],
                                     ps[4 + s][:, :].rearrange("p (k t) -> p k t", k=4), ACT.Copy).then_inc(yT_a, 1)
            act.wait_ge(conv_ready, 2)
            nc.scalar.activation(xT_hi[:, 4:8, :], conv[:, 4:8, :], ACT.Copy).then_inc(conv_a, 1)
            hi_quarters(14 * RING + 2, 15 * RING)
            hi_blocks(15, 18)
            hi_quarters(WQ0 * RING, WQ0 * RING + 2)

            act.wait_ge(free_v, 4 + 36)
            for t in range(TT):
                mean_square(t)
            transposes_hi(1)

            def queries(m):
                if m >= 2:
                    act.wait_ge(scores_mm, m - 1)
                act.wait_ge(half_used, through(WQ0 + m))
                for j in range(2):
                    nc.scalar.activation(q_heads[m % 2][:, 2 * j:2 * j + 2, :].rearrange("p c t -> p (c t)"),
                                         ps[2 * (m % 2) + j][:, :], ACT.Copy).then_inc(q_out, 1)

            def scores(m):
                act.wait_ge(scores_mm, m + 1)
                if m == 2:
                    act.wait_ge(scores_used, 1)
                late = m == BLOCKS_WQ - 1
                nc.scalar.activation((scores1[:, 0:4, :] if late else scores0[:, m % 2, :, :])
                                     .rearrange("p c n -> p (c n)"), ps[4 + 2 * (m % 2)][:, :], ACT.Copy)
                nc.scalar.activation(scores1[:, 4 * m + 4:4 * m + 8, :].rearrange("p c n -> p (c n)"),
                                     ps[5 + 2 * (m % 2)][:, :], ACT.Copy).then_inc(scores_out, 1)

            q0 = WQ0 * RING
            for m in (0, 2):
                at_m = q0 + RING * m + 2
                hi_quarters(at_m, at_m + RING)
                queries(m)
                hi_quarters(at_m + RING, at_m + RING + 1)
                scores(m)
                hi_quarters(at_m + RING + 1, at_m + 2 * RING)
                queries(m + 1)
                scores(m + 1)

            def gates_of(first, heads):
                act.wait_ge(below_ready, 2 if first else 1)
                nc.scalar.activation(gate[:, first * TOPK:(first + heads) * TOPK], below_top[:, 0:heads * TOPK],
                                     ACT.Exp).then_inc(gate_exp, 1)

            def group(par, g):
                act.wait_ge(u_used, g * G + 2 * G)
                nc.scalar.activation(act_now[par][:, :], dots[par][:, :], ACT.Gelu).then_inc(act_ready, 1)

            gates_of(0, EARLY)
            act.wait_ge(scores_out, 2 + BLOCKS_WQ)
            for t in range(TT):
                if t == 0:
                    with act.Fori(0, UNITS // 2) as i:
                        for par in range(2):
                            g = i * 2 + par
                            act.wait_ge(now_used, g + 1)
                            nc.scalar.activation(scores_now[:, :, :], scores1[:, bass.ds(i * 4 + 2 * par, 2), :],
                                                 ACT.Copy).then_inc(now_ready, 1)
                            group(par, g)
                    gates_of(EARLY, UNITS)
                with act.Fori(UNITS // 2 if t == 0 else 0, GROUPS // 2) as i:
                    for par in range(2):
                        group(par, i * 2 + (t * GROUPS + par))
                act.wait_ge(v_used, G + (t + 1) * SLOTS)
                for n in range(4):
                    nc.scalar.activation(h[:, t, n * NB:(n + 1) * NB], ps[4 * t + n][:, :], ACT.Copy)\
                        .then_inc(peer_out, 1)
            act.wait_ge(peer_out, 4 * TT)
            for t in range(TT):
                mean_square(t)
            transposes_hi(2)

            def last_gate(m):
                act.wait_ge(half_used, through(PLE0 + m))
                if m >= 2:
                    act.wait_ge(ple_added, 2 * (m - 1))
                for t in range(TT):
                    nc.scalar.activation(sig[m % 2][t], ps[2 * (m % 2) + t][:, :], ACT.Sigmoid).then_inc(sig_out, 1)

            q0 = PLE0 * RING
            hi_quarters(q0 + 2, q0 + RING + 2)
            for m in range(BLOCKS_PLE):
                last_gate(m)
                hi_quarters(q0 + RING * (m + 1) + 2, min(q0 + RING * (m + 2) + 2, q0 + RING * BLOCKS_PLE))

            act.wait_ge(ple_added, 2 * BLOCKS_PLE)
            for t in range(TT):
                mean_square(t)

        @block.vector
        def _(dve):
            step = Count(dve, dve_c)
            v = nc.vector

            def normalise(norm):
                for t in range(TT):
                    dve.wait_ge(sq_done, norm * TT + t + 1)
                    step.done(v.reciprocal(rstd[:, t:t + 1], root[:, t:t + 1]))
                    step.wait()
                    if t == 0:
                        dve.wait_ge(final_in if norm == 3 else gain_in[norm], 16)
                    v.scalar_tensor_tensor(out=xn[:, t, :], in0=h[:, t, :], scalar=rstd[:, t:t + 1],
                                           in1=fin_rows if norm == 3 else g_rows, op0=ALU.mult, op1=ALU.mult)\
                        .then_inc(out_ready if norm == 3 else xn_ready, 1)

            def transposes_lo(norm):
                for s in range(8):
                    dve.wait_ge(xT_a, norm * 8 + s + 1)
                    to = slice(s % 4 * 4, s % 4 * 4 + 4), slice(s // 4 * P, (s // 4 + 1) * P)
                    v.tensor_tensor(xT_lo[:, to[0], to[1]], ps[4 + s % 4][:, :].rearrange("p (k t) -> p k t", k=4),
                                    xT_hi[:, to[0], to[1]].bitcast(F32), ALU.subtract).then_inc(xT_v, 1)

            def empty_channels(dst, n, scale=None):
                b = n % 2
                dve.wait_ge(half_used, through(n))
                for j in range(2):
                    to = dst[:, 4 * b + 2 * j:4 * b + 2 * j + 2, :].rearrange("p c t -> p (c t)")
                    if scale is None:
                        v.tensor_copy(to, ps[2 * b + j][:, :]).then_inc(free_v, 1)
                    else:
                        v.tensor_scalar(to, ps[2 * b + j][:, :], scale, None, ALU.mult).then_inc(free_v, 1)

            normalise(0)
            dve.wait_ge(gw_a, 1)
            v.tensor_tensor(gw_lo[:, :, :], gw[:, :, :], gw_hi[:, :, :].bitcast(F32), ALU.subtract).then_inc(gw_v, 1)
            transposes_lo(0)

            dve.wait_ge(small_in[1], 16)
            dve.wait_ge(setup_mm, 1)
            step.done(v.tensor_tensor(gates[:, :, :], ps[4][:, 0:16].rearrange("p (a n) -> p a n", a=TT),
                                      gb[:, :].unsqueeze(1).to_broadcast([P, TT, 2 * H]), ALU.add))
            step.wait()
            v.scalar_tensor_tensor(out=abs_f[:, :, :], in0=gates[:, :, H:2 * H], scalar=-1.0, in1=gates[:, :, H:2 * H],
                                   op0=ALU.mult, op1=ALU.max).then_inc(abs_ready, 1)
            dve.wait_ge(setup_mm, 2)
            v.tensor_copy(cols[:, :, :].rearrange("p j c -> p (j c)"), ps[5][:, 0:TAPS * CT]).then_inc(setup_v, 1)
            dve.wait_ge(setup_mm, 3)
            v.tensor_copy(pT[:, :, :].rearrange("p k t -> p (k t)"), ps[6][:, :]).then_inc(setup_v, 1)
            for n, bank in enumerate((7, 5, 6, 7)):
                dve.wait_ge(setup_mm, 4 + n)
                v.tensor_copy(keysT[:, 4 * n:4 * n + 4, :].rearrange("p a n -> p (a n)"), ps[bank][:, :])\
                    .then_inc(setup_v, 1)
            dve.wait_ge(softplus, 1)
            v.scalar_tensor_tensor(out=lf[:, :, :], in0=gates[:, :, H:2 * H], scalar=0.0, in1=log_f[:, :, :],
                                   op0=ALU.min, op1=ALU.subtract).then_inc(lf_ready, 1)
            dve.wait_ge(setup_mm, 8)
            step.done(v.tensor_copy(bcum[:, :, :].rearrange("p a h -> p (a h)"), ps[4][:, 256:264]))
            step.wait()
            step.done(v.tensor_tensor(e_in[:, :, :], gates[:, :, 0:H], bcum[:, :, :], ALU.subtract))
            step.wait()
            for a in range(TT):
                for hh in range(H):
                    last = v.tensor_scalar(diag_e[:, a * H + hh, :], ident[:, :], e_in[:, a, hh:hh + 1], None, ALU.mult)
            last.then_inc(diag_e_ready, 1)

            for n in range(2):
                empty_channels(qT, n)
            for n in range(2, 4):
                empty_channels(kT, n, scale=HD ** -0.5)

            dve.wait_ge(mix_mm, 1)
            for a in range(TT):
                for hh in range(H):
                    step.done(v.scalar_tensor_tensor(
                        out=pw[:, a * H + hh, :], in0=ps[4 + a][:, hh * P:(hh + 1) * P],
                        scalar=bcum[:, a, hh:hh + 1], in1=mask[:, :], op0=ALU.add, op1=ALU.add))
            step.wait()
            step.done(v.tensor_reduce(m_in[:, :, :].rearrange("p a h -> p (a h)"), pw, axis=AX.X, op=ALU.max))
            step.wait()
            step.done(v.tensor_tensor(m_t[:, 0, :], bcum[:, 0, :], m_in[:, 0, :], ALU.max))
            step.done(v.tensor_tensor(mb[:, 0:H], bcum[:, 0, :], m_in[:, 0, :], ALU.max))
            v.tensor_copy(mb[:, H:2 * H], bcum[:, 0, :]).then_inc(mb_ready, 1)
            dve.wait_ge(mix_mm, 3)
            step.done(v.tensor_copy(mb_last[:, :], ps[4][:, 0:2 * H]))
            step.wait()
            step.done(v.tensor_tensor(inter[:, :], bcum[:, 1, :], mb_last[:, 0:H], ALU.add))
            step.done(v.tensor_tensor(decay[:, 0, :], mb_last[:, H:2 * H], mb_last[:, 0:H], ALU.subtract))
            step.wait()
            step.done(v.tensor_tensor(m_t[:, 1, :], inter[:, :], m_in[:, 1, :], ALU.max))
            step.done(v.tensor_tensor(decay[:, 0, :], decay[:, 0, :], e_in[:, 0, :], ALU.add))
            step.wait()
            step.done(v.tensor_scalar(neg_m[:, :, :], m_t[:, :, :], -1.0, None, ALU.mult))
            v.tensor_tensor(decay[:, 1, :], inter[:, :], m_t[:, 1, :], ALU.subtract).then_inc(m_ready, 1)

            for n in range(4, 6):
                dve.wait_ge(half_used, through(n))
                for t in range(TT):
                    v.tensor_copy(vS[:, t, 2 * (n % 2):2 * (n % 2) + 2, 0:HD],
                                  ps[2 * (n % 2) + t][:, :].rearrange("p (h e) -> p h e", h=2)).then_inc(free_v, 1)
            dve.wait_ge(pw_ready, 1)
            dve.wait_ge(mix_mm, 2)
            for a in range(TT):
                last = v.tensor_tensor(pw[:, a * H:(a + 1) * H, :], ps[6 + a][:, :].rearrange("p (h s) -> p h s", h=H),
                                       pw[:, a * H:(a + 1) * H, :], ALU.mult)
            last.then_inc(sc_ready, 1)
            for n in range(6, 8):
                dve.wait_ge(half_used, through(n))
                for t in range(TT):
                    v.tensor_copy(o_sig[:, t, n % 2 * NB:(n % 2 + 1) * NB], ps[2 * (n % 2) + t][:, :])\
                        .then_inc(free_v, 1)

            dve.wait_ge(mix_mm, 5)
            for a in range(TT):
                last = v.tensor_copy(scT[:, a * H:(a + 1) * H, :].rearrange("p h t -> p (h t)"), ps[6 + a][:, :])
            last.then_inc(scT_ready, 1)
            for hh in range(H):
                last = v.tensor_scalar(kN[:, hh, :], ps[4 + hh // 2][:, hh % 2 * HD:(hh % 2 + 1) * HD],
                                       decay[:, 0, hh:hh + 1], None, ALU.mult)
            last.then_inc(kN_ready, 1)
            for hh in range(H):
                dve.wait_ge(bank_mm, 4 + 2 * hh + 2)
                v.tensor_copy(state[:, hh, 1, :], ps[(5 + 2 * hh) % 8][:, 0:HW]).then_inc(bank_v, 1)
            dve.wait_ge(bank_a, 12)
            for hh in range(H):
                dve.wait_ge(bank_mm, 16 + hh + 1)
                v.scalar_tensor_tensor(out=num[:, 1, hh, :], in0=ps[hh][:, 0:HW], scalar=decay[:, 1, hh:hh + 1],
                                       in1=num[:, 1, hh, :], op0=ALU.mult, op1=ALU.add).then_inc(bank_v, 1)
            dve.wait_ge(bank_v, 8)
            step.done(v.scalar_tensor_tensor(out=den[:, :, :], in0=num[:, :, :, HD], scalar=-1.0,
                                             in1=num[:, :, :, HD], op0=ALU.mult, op1=ALU.max))
            step.wait()
            step.done(v.tensor_tensor(den[:, :, :], den[:, :, :], floor[:, :, :], ALU.max))
            step.wait()
            v.reciprocal(rden[:, :, :], den[:, :, :]).then_inc(rden_ready, 1)
            dve.wait_ge(o_out, 1)
            dve.wait_ge(small_in[3], 16)
            step.done(v.tensor_tensor(o_sig, o_sig, o_gain.unsqueeze(1).to_broadcast([P, TT, CONV]), ALU.mult))
            dve.wait_ge(head_rt, 1)
            step.done(v.reciprocal(head_scale[:, :, :], head_root[:, :, :]))
            step.wait()
            step.done(v.tensor_tensor(head_scale[:, :, :], head_scale[:, :, :], rden[:, :, :], ALU.mult))
            step.wait()
            for a in range(TT):
                for hh in range(H):
                    last = v.scalar_tensor_tensor(
                        out=o_sig[:, a, hh * HD:(hh + 1) * HD], in0=num[:, a, hh, 0:HD],
                        scalar=head_scale[:, a, hh:hh + 1], in1=o_sig[:, a, hh * HD:(hh + 1) * HD],
                        op0=ALU.mult, op1=ALU.mult)
            last.then_inc(y_ready, 1)
            dve.wait_ge(y_ready, 1)

            for n in range(8, 10):
                empty_channels(bT, n)
            for n in range(10, 12):
                empty_channels(zT, n)
            dve.wait_ge(free_v, 4 + 24)
            for n in range(12, 14):
                b = n % 2
                dve.wait_ge(half_used, through(n))
                for j in range(2):
                    zz = zT[:, 4 * b + 2 * j:4 * b + 2 * j + 2, :].rearrange("p c t -> p (c t)")
                    v.tensor_tensor(zz, ps[2 * b + j][:, :], zz, ALU.mult).then_inc(free_v, 1)
                dve.wait_ge(free_v, 4 + 2 * (n + 1))
                mine = range(4 * b, 4 * b + 4)
                for c in mine:
                    step.done(v.tensor_scalar(conv[:, c, :], zT[:, c, :], cols[:, 2, c:c + 1], None, ALU.mult))
                step.wait()
                for back in (1, 2):
                    for c in mine:
                        step.done(v.scalar_tensor_tensor(
                            out=conv[:, c, back:S], in0=zT[:, c, 0:S - back], scalar=cols[:, 2 - back, c:c + 1],
                            in1=conv[:, c, back:S], op0=ALU.mult, op1=ALU.add))
                    step.wait()
                four = slice(4 * b, 4 * b + 4)
                v.tensor_tensor(conv[:, four, :], conv[:, four, :], bT[:, four, :], ALU.mult).then_inc(conv_ready, 1)
                if b == 0:
                    dve.wait_ge(conv_a, 1)
                    v.tensor_tensor(xT_lo[:, four, :], conv[:, four, :], xT_hi[:, four, :].bitcast(F32),
                                    ALU.subtract).then_inc(conv_v, 1)
            for s in range(4):
                dve.wait_ge(yT_a, s + 1)
                c, to = CT + s % 2 * 4, slice(s // 2 * P, (s // 2 + 1) * P)
                v.tensor_tensor(xT_lo[:, c:c + 4, to], ps[4 + s][:, :].rearrange("p (k t) -> p k t", k=4),
                                xT_hi[:, c:c + 4, to].bitcast(F32), ALU.subtract).then_inc(yT_v, 1)
            dve.wait_ge(conv_a, 2)
            v.tensor_tensor(xT_lo[:, 4:8, :], conv[:, 4:8, :], xT_hi[:, 4:8, :].bitcast(F32), ALU.subtract)\
                .then_inc(conv_v, 1)

            for n in range(BLOCKS_OUT):
                b = n % 2
                dve.wait_ge(half_used, through(OUT0 + n))
                for t in range(TT):
                    hh = h[:, t, n * NB:(n + 1) * NB]
                    v.tensor_tensor(hh, ps[2 * b + t][:, :], hh, ALU.add).then_inc(free_v, 1)

            normalise(1)
            transposes_lo(1)

            def top16(lists):
                for part in (slice(0, 8), slice(8, 16)):
                    for s, _, src in lists:
                        step.done(v.max(s[:, part], src))
                    step.wait_apart(passed_v)
                    for s, n, src in lists:
                        step.done(v.max_index(n[:, part], s[:, part], src))
                    step.wait_apart(passed_v)
                    if part.start == 0:
                        for s, _, src in lists:
                            step.done(v.match_replace(src, s[:, part], src, FAR))
                        step.wait_apart(passed_v)

            def top_experts(heads, source, cand, hot, to):
                n = heads
                top16([(top_s[:, a, e, :], top_i[:, a, e, :], source(a, e)) for a in range(n) for e in range(2)])
                wide = [P, n, TOPK, TOPK]
                step.done(v.tensor_copy(top_f[:, 0:n, :, :].rearrange("p h e k -> p (h e k)"),
                                        top_i[:, 0:n, :, :].rearrange("p h e k -> p (h e k)")))
                step.done(v.tensor_tensor(cand.rearrange("p h (a b) -> p h a b", a=TOPK),
                                          top_s[:, 0:n, 0, :].unsqueeze(3).to_broadcast(wide),
                                          top_s[:, 0:n, 1, :].unsqueeze(2).to_broadcast(wide), ALU.add))
                step.wait_apart(passed_v)
                top16([(best[:, a, :], pos[:, a, :], cand[:, a, :]) for a in range(n)])
                step.done(v.tensor_scalar(pos_a[:, 0:n, :], pos[:, 0:n, :], 4, None, ALU.logical_shift_right))
                step.done(v.tensor_scalar(pos_b[:, 0:n, :], pos[:, 0:n, :], TOPK - 1, None, ALU.bitwise_and))
                step.done(v.tensor_copy(gate[:, bass.ds(to, n * TOPK)],
                                        best[:, 0:n, :].rearrange("p h k -> p (h k)")))
                step.wait()
                step.done(v.tensor_copy(pos_f[0][:, 0:n, :], pos_a[:, 0:n, :]))
                step.done(v.tensor_copy(pos_f[1][:, 0:n, :], pos_b[:, 0:n, :]))
                step.wait()
                for e in range(2):
                    step.done(v.tensor_tensor(hot, pos_f[e][:, 0:n, :].unsqueeze(3).to_broadcast(wide),
                                              iota16[:, :].unsqueeze(1).unsqueeze(1).to_broadcast(wide),
                                              ALU.is_equal))
                    step.wait()
                    step.done(v.tensor_tensor(hot, hot, top_f[:, 0:n, e, :].unsqueeze(2).to_broadcast(wide), ALU.mult))
                    step.wait()
                    step.done(v.tensor_reduce(sel[e][:, 0:n, :], hot, axis=AX.X, op=ALU.add))
                    step.wait()
                step.done(v.scalar_tensor_tensor(out=expert[:, bass.ds(to, n * TOPK)],
                                                 in0=sel[0][:, 0:n, :].rearrange("p h k -> p (h k)"), scalar=float(NK),
                                                 in1=sel[1][:, 0:n, :].rearrange("p h k -> p (h k)"),
                                                 op0=ALU.mult, op1=ALU.add))
                step.wait_apart(passed_v)

            def softmax(first, heads):
                wide = [P, heads, TOPK]
                per_head = gate[:, first * TOPK:(first + heads) * TOPK].rearrange("p (n k) -> p n k", k=TOPK)
                sums, inv = gate_sum[:, first:first + heads], gate_inv[:, first:first + heads]
                v.tensor_tensor(below_top[:, 0:heads * TOPK].rearrange("p (n k) -> p n k", k=TOPK), per_head,
                                per_head[:, :, 0:1].to_broadcast(wide), ALU.subtract).then_inc(below_ready, 1)
                dve.wait_ge(gate_exp, 2 if first else 1)
                step.done(v.tensor_reduce(sums, per_head, axis=AX.X, op=ALU.add))
                step.wait()
                step.done(v.reciprocal(inv, sums))
                step.wait()
                step.done(v.tensor_tensor(per_head, per_head, inv.unsqueeze(2).to_broadcast(wide), ALU.mult))
                step.wait()

            dve.wait_ge(consts, 5)
            dve.wait_ge(pool_c, 6)
            for m in range(EARLY // 2):
                dve.wait_ge(scores_out, 2 + (m + 1))
                dve.sem_inc(passed_v, 1)
                top_experts(2, lambda a, e: scores0[:, m % 2, 2 * a + e, :],
                            tmp[:, 0:2 * CAND].rearrange("p (h c) -> p h c", h=2),
                            tmp[:, 2 * CAND:4 * CAND].rearrange("p (h k a) -> p h k a", h=2, k=TOPK),
                            2 * m * TOPK)
                if m == 0:
                    v.tensor_copy(idx_now[0][:, :], expert[:, 0:G]).then_inc(idx_ready, 1)
                dve.sem_inc(scores_used, 1)
            softmax(0, EARLY)

            def group(t, par, g):
                v.tensor_copy(gate_now[par][:, :], gate[:, bass.ds(g * G, G)]).then_inc(gate_c, 1)
                for s in range(G):
                    dve.wait_ge(u_in[s], g * 16 + 16)
                    v.tensor_tensor_reduce(out=u_rows[s], in0=u_rows[s], in1=xn[:, t, :], scale=1.0,
                                           scalar=0.0, op0=ALU.mult, op1=ALU.add,
                                           accum_out=dots[par][:, s:s + 1]).then_inc(u_used, 1)
                dve.wait_ge(v_used, g * G + G)
                v.tensor_copy(idx_now[1 - par][:, :], expert[:, bass.ds(g * G + G, G)]).then_inc(idx_ready, 1)
                dve.wait_ge(act_ready, g + 1)
                dve.wait_ge(gate_c, g + 1)
                for s in range(G):
                    dve.wait_ge(v_used, g * G + (s + 1))
                    v.tensor_scalar(v_diag[s], ident[:, :], act_now[par][:, s:s + 1],
                                    gate_now[par][:, s:s + 1], ALU.mult, ALU.mult).then_inc(diag_ready, 1)

            for t in range(TT):
                if t == 0:
                    base, first = step.n, step.steps
                    with dve.Fori(0, UNITS // 2) as i:
                        for par in range(2):
                            g = i * 2 + par
                            group(t, par, g)
                            step.n = i * (2 * UNIT_STEPS) + (base + par * UNIT_STEPS)
                            dve.wait_ge(now_ready, g + 1)
                            dve.sem_inc(passed_v, 1)
                            top_experts(1, lambda a, e: scores_now[:, e, :],
                                        tmp[:, 512:512 + CAND].rearrange("p (h c) -> p h c", h=1),
                                        tmp[:, 768:768 + CAND].rearrange("p (h k a) -> p h k a", h=1, k=TOPK),
                                        i * (2 * TOPK) + (EARLY + par) * TOPK)
                            dve.sem_inc(now_used, 1)
                    assert step.steps - first == 2 * UNIT_STEPS, step.steps - first
                    step.n = base + UNITS * UNIT_STEPS
                    softmax(EARLY, UNITS)
                with dve.Fori(UNITS // 2 if t == 0 else 0, GROUPS // 2) as i:
                    for par in range(2):
                        group(t, par, i * 2 + (t * GROUPS + par))

            normalise(2)
            transposes_lo(2)
            for n in range(BLOCKS_PLE):
                b = n % 2
                dve.wait_ge(ple_mm, n + 1)
                dve.wait_ge(sig_out, 4 + 2 * (n + 1))
                for t in range(TT):
                    v.tensor_tensor(sig[b][t], ps[4 + 2 * b + t][:, :], sig[b][t], ALU.mult).then_inc(ple_used, 1)
                dve.wait_ge(ple_used, 4 + 2 * (n + 1))
                for t in range(TT):
                    hh = h[:, t, n * NB:(n + 1) * NB]
                    v.tensor_tensor(hh, hh, sig[b][t], ALU.add).then_inc(ple_added, 1)
            normalise(3)


_VIEWS = {
    "x": (S, D), "p": (S, PLE), "norm_mix_g": (1, D), "w_in": (D, GATES_AT + 2 * H), "conv_w": (TAPS, CONV),
    "mlstm_gate_b": (1, 2 * H), "mlstm_norm_g": (1, H * HD), "w_out": (D, D), "norm_ffn_g": (1, D),
    "peer_wq": (D, D), "peer_keys": (2 * PH, NK, P), "peer_u": (NK * NK, D), "peer_v": (NK * NK, D),
    "norm_ple_g": (1, D), "ple_w_gate": (D, D), "ple_w_proj": (PLE, D), "norm_final_g": (1, D),
}


def kernel(**inputs):
    import numpy as _np
    import concourse.bacc as _bacc
    from concourse import mybir as _mybir
    from concourse.bass_utils import run_bass_kernel_spmd as _run

    nc = _bacc.Bacc("TRN2", target_bir_lowering=False, num_devices=1)
    arrays, args = {}, []
    for name, shape in _VIEWS.items():
        a = _np.ascontiguousarray(inputs[name]).reshape(shape)
        arrays[f"in_{name}"] = a
        args.append(nc.dram_tensor(f"in_{name}", shape, _mybir.dt.from_np(a.dtype), kind="ExternalInput").ap())
    args.append(nc.dram_tensor("out_h", (S, D), F32, kind="ExternalOutput").ap())
    build(nc, *args)
    r = _run(nc, [arrays], core_ids=[0])
    return r.results[0]["out_h"].reshape(1, S, D)
```

```python
from contextlib import ExitStack

import concourse.bass as bass
from concourse import mybir

F32 = mybir.dt.float32
F32R = mybir.dt.float32r
U32 = mybir.dt.uint32
ALU = mybir.AluOpType
ACT = mybir.ActivationFunctionType
AX = mybir.AxisListType

P = 128
D = 2048
S = 256
TT = S // P
KT = D // P
KQ = KT // 4
NB = 512
CONV = 1024
TAPS = 3
H, HD = 4, 256
HW = HD + 1
CT = CONV // P
PH, TOPK, NK = 8, 16, 128
CAND = TOPK * TOPK
SLOTS = PH * TOPK
PLE = 256
PT = PLE // P
EPS = 1e-6
FAR = -3.0e38
G = 4
GROUPS = SLOTS // G
RING = 4
KH = KQ // 2
HALVES = 2
SPLIT = 4
EARLY = 4
UNITS = TT * PH - EARLY
UNIT_STEPS = 29
Q_AT, B_AT, GATES_AT = 3072, 0, 7168
BLOCKS_OUT, BLOCKS_WQ, BLOCKS_PLE = 4, 4, 4


class Count:

    def __init__(self, engine, sem):
        self.engine, self.sem, self.n, self.steps = engine, sem, 0, 0

    def done(self, instruction):
        instruction.then_inc(self.sem, 1)
        self.n, self.steps = self.n + 1, self.steps + 1

    def wait(self):
        self.engine.wait_ge(self.sem, self.n)

    def wait_apart(self, passed):
        self.wait()
        self.engine.sem_inc(passed, 1)


def build(nc, x, p, g_mix, w_in, conv_w, gate_b, g_mlstm, w_out, g_ffn, wq, keys, u_tab, v_tab,
          g_ple, w_gate, w_proj, g_final, out):
    ctx = ExitStack()
    with ctx:
        def sb(name, shape, dt=F32):
            return ctx.enter_context(nc.sbuf_tensor(name, shape, dt))

        def sem(name):
            return ctx.enter_context(nc.semaphore(name))

        w_hi = [sb(f"w_hi{i}", [P, KH, NB], F32R) for i in range(SPLIT)]
        w_lo = [sb(f"w_lo{i}", [P, KH, NB], F32R) for i in range(SPLIT)]
        h = sb("h", [P, TT, D])
        xn = sb("xn", [P, TT, D])
        xT_hi = sb("xT_hi", [P, KT, S], F32R)
        xT_lo = sb("xT_lo", [P, KT, S], F32R)
        pT = sb("pT", [P, PT, S])
        big = sb("big", [P, 2 * G * D + 24])

        at = [0]

        def view(size, pattern, **sizes):
            v = big[:, at[0]:at[0] + size].rearrange(pattern, **sizes)
            at[0] += size
            return v

        bT = view(CT * S, "p (c t) -> p c t", t=S)
        zT = view(CT * S, "p (c t) -> p c t", t=S)
        at[0] += 4 * H * HW - 2 * CT * S
        qT = view(CT * S, "p (c t) -> p c t", t=S)
        kT = view(CT * S, "p (c t) -> p c t", t=S)
        vS = view(TT * H * HW, "p (a h e) -> p a h e", a=TT, h=H)
        keysT = view(2 * PH * NK, "p (a n) -> p a n", n=NK)
        raw = [sb(f"raw{i}", [P, KQ, NB])[:, :, :] for i in range(2)] + \
            [view(KQ * NB, "p (k n) -> p k n", k=KQ) for i in range(2)]
        conv = qT
        o_sig = xn[:, 0, :].rearrange("p (a n) -> p a n", a=TT)
        state = big[:, 0:2 * H * HW].rearrange("p (h d e) -> p h d e", h=H, d=2)
        num = big[:, 2 * H * HW:4 * H * HW].rearrange("p (a h e) -> p a h e", a=TT, h=H)
        keys_raw = qT.rearrange("p c t -> p (c t)").rearrange("p (a c) -> p a c", c=P)
        p_raw = big[:, CT * S:CT * S + TT * PLE].rearrange("p (a c) -> p a c", a=TT)
        u_rows = [big[:, i * D:(i + 1) * D] for i in range(G)]
        v_rows = [big[:, (G + i) * D:(G + i + 1) * D] for i in range(G)]
        g_rows = u_rows[0]
        wp = big[:, 2 * D:2 * D + PT * D].rearrange("p (k n) -> p k n", k=PT)
        q_heads = [v_rows[0][:, i * 4 * S:(i + 1) * 4 * S].rearrange("p (c t) -> p c t", t=S)
                   for i in range(2)]
        sig = [[v_rows[0][:, (2 * b + t) * NB:(2 * b + t + 1) * NB] for t in range(TT)] for b in range(2)]

        scores0 = sb("scores0", [P, 2, 4, NK])
        scores1 = sb("scores1", [P, 2 * UNITS, NK])
        ple_rows = scores1[:, 0:D // NK, :].rearrange("p a n -> p (a n)")
        tmp = sb("tmp", [P, 1024])
        pw = scores0[:, :, :, :].rearrange("p a h s -> p (a h) s")
        diag_e = scores1[:, 0:TT * H, :]
        scT = diag_e
        o_gain = scores1[:, TT * H:2 * TT * H, :].rearrange("p a n -> p (a n)")
        kN = tmp[:, :].rearrange("p (h d) -> p h d", h=H)
        v_diag = [tmp[:, i * P:(i + 1) * P] for i in range(G)]
        below_top = tmp[:, 512:512 + UNITS * TOPK]

        ident = sb("ident", [P, P])
        mix_consts = sb("mix_consts", [P, 2, P])
        tri = mix_consts[:, 0, :]
        last_row = mix_consts[:, 1, :]
        scores_now = mix_consts
        mask = sb("mask", [P, P])
        ones = sb("ones", [P, P])
        stack = sb("stack", [TAPS * CT, P])
        cols = sb("cols", [P, TAPS, CT])
        gw = tmp[:, 256:256 + KT * 2 * H].rearrange("p (k n) -> p k n", k=KT)
        gw_split = sb("gw_split", [P, KT, 2, 2 * H], F32R)
        gT = tmp[0:4 * H, 0:S]
        gb = sb("gb", [P, 2 * H])
        eps = sb("eps", [P, 1])
        sq_part = sb("sq_part", [P, TT, 4])
        sq_sum = sb("sq_sum", [P, TT])
        root = sb("root", [P, TT])
        rstd = sb("rstd", [P, TT])
        unused = sb("unused", [P, 1])
        gates = sb("gates", [P, TT, 2 * H])
        abs_f = sb("abs_f", [P, TT, H])
        exp_f = sb("exp_f", [P, TT, H])
        log_f = sb("log_f", [P, TT, H])
        lf = sb("lf", [P, TT, H])
        bcum = sb("bcum", [P, TT, H])
        e_in = sb("e_in", [P, TT, H])
        m_in = sb("m_in", [P, TT, H])
        m_t = sb("m_t", [P, TT, H])
        neg_m = sb("neg_m", [P, TT, H])
        mb = sb("mb", [P, 2 * H])
        mb_last = sb("mb_last", [P, 2 * H])
        inter = sb("inter", [P, H])
        decay = sb("decay", [P, 2, H])
        floor = sb("floor", [P, TT, H])
        den = sb("den", [P, TT, H])
        rden = sb("rden", [P, TT, H])
        head_sq = sb("head_sq", [P, TT, H])
        head_root = sb("head_root", [P, TT, H])
        head_scale = sb("head_scale", [P, TT, H])

        iota16 = sb("iota16", [P, TOPK])
        top_s = sb("top_s", [P, 2, 2, TOPK])
        top_i = sb("top_i", [P, 2, 2, TOPK], U32)
        top_f = sb("top_f", [P, 2, 2, TOPK])
        best = sb("best", [P, 2, TOPK])
        pos = sb("pos", [P, 2, TOPK], U32)
        pos_a = sb("pos_a", [P, 2, TOPK], U32)
        pos_b = sb("pos_b", [P, 2, TOPK], U32)
        pos_f = [sb(f"pos_f{i}", [P, 2, TOPK]) for i in range(2)]
        sel = [sb(f"sel{i}", [P, 2, TOPK]) for i in range(2)]
        expert = sb("expert", [P, TT * SLOTS + 2 * G], U32)
        gate = sb("gate", [P, TT * SLOTS])
        gate_sum = sb("gate_sum", [P, TT * PH])
        gate_inv = sb("gate_inv", [P, TT * PH])
        idx_u = [sb(f"idx_u{i}", [P, G], U32) for i in range(2)]
        idx_v = [sb(f"idx_v{i}", [P, G], U32) for i in range(2)]
        gate_now = [sb(f"gate_now{i}", [P, G]) for i in range(2)]
        dots = [sb(f"dots{i}", [P, G]) for i in range(2)]
        act_now = [sb(f"act_now{i}", [P, G]) for i in range(2)]

        ps = [ctx.enter_context(nc.psum_tensor(f"ps{i}", [P, NB], F32)) for i in range(8)]

        x_in = [sem(f"x_in{t}") for t in range(TT)]
        small_in = [sem(f"small_in{i}") for i in range(6)]
        gain_in = [sem(f"gain_in{i}") for i in range(3)]
        final_in = sem("final_in")
        wp_in = sem("wp_in")
        raw_in = [sem(f"raw_in{i}") for i in range(RING)]
        hi_ready = sem("hi_ready")
        lo_ready = sem("lo_ready")
        half_used = sem("half_used")
        consts = sem("consts")
        free_v = sem("free_v")
        sq_parts = sem("sq_parts")
        sum_ready = sem("sum_ready")
        sq_done = sem("sq_done")
        xn_ready = sem("xn_ready")
        tr_mm = sem("tr_mm")
        xT_a = sem("xT_a")
        xT_v = sem("xT_v")
        gw_a = sem("gw_a")
        gw_v = sem("gw_v")
        gT_mm = sem("gT_mm")
        gT_v = sem("gT_v")
        gates_mm = sem("gates_mm")
        setup_mm = sem("setup_mm")
        setup_v = sem("setup_v")
        abs_ready = sem("abs_ready")
        softplus = sem("softplus")
        lf_ready = sem("lf_ready")
        diag_e_ready = sem("diag_e_ready")
        mix_mm = sem("mix_mm")
        mb_ready = sem("mb_ready")
        m_ready = sem("m_ready")
        pw_ready = sem("pw_ready")
        sc_ready = sem("sc_ready")
        kN_ready = sem("kN_ready")
        scT_ready = sem("scT_ready")
        bank_mm = sem("bank_mm")
        bank_a = sem("bank_a")
        bank_v = sem("bank_v")
        o_out = sem("o_out")
        rden_ready = sem("rden_ready")
        head_rt = sem("head_rt")
        y_ready = sem("y_ready")
        yT_mm = sem("yT_mm")
        yT_a = sem("yT_a")
        yT_v = sem("yT_v")
        conv_ready = sem("conv_ready")
        conv_a = sem("conv_a")
        conv_v = sem("conv_v")
        q_out = sem("q_out")
        scores_mm = sem("scores_mm")
        scores_out = sem("scores_out")
        now_ready = sem("now_ready")
        now_used = sem("now_used")
        below_ready = sem("below_ready")
        gate_exp = sem("gate_exp")
        idx_u_ready = sem("idx_u_ready")
        idx_v_ready = sem("idx_v_ready")
        gate_c = sem("gate_c")
        u_in = [sem(f"u_in{i}") for i in range(G)]
        v_in = [sem(f"v_in{i}") for i in range(G)]
        u_used = sem("u_used")
        v_used = sem("v_used")
        act_ready = sem("act_ready")
        diag_ready = sem("diag_ready")
        peer_out = sem("peer_out")
        ple_mm = sem("ple_mm")
        gate_mm = sem("gate_mm")
        sig_out = sem("sig_out")
        ple_used = sem("ple_used")
        ple_added = sem("ple_added")
        out_ready = sem("out_ready")
        stored = [sem(f"stored{t}") for t in range(TT)]
        act_c = sem("act_c")
        dve_c = sem("dve_c")
        pool_c = sem("pool_c")
        passed_v, passed_p, passed_s = sem("passed_v"), sem("passed_p"), sem("passed_s")

        OUT0, WQ0, PLE0 = 14, 18, 22
        Y_STEPS = (0, 2, 1, 3)
        ORDER_IN, ORDER_OUT = (0, 1, 2, 3), (2, 3, 0, 1)

        def through(n):
            return SPLIT + HALVES * RING * (n + 1)

        block = ctx.enter_context(nc.Block())

        @block.sync
        def _(sp):
            sp.dma_start(h[:, 0, :], x[0:P, :]).then_inc(x_in[0], 16)
            sp.dma_start(g_rows, g_mix.to_broadcast([P, D])).then_inc(gain_in[0], 16)
            sp.dma_start(h[:, 1, :], x[P:2 * P, :]).then_inc(x_in[1], 16)
            sp.dma_start(gw, w_in[:, GATES_AT:GATES_AT + 2 * H].rearrange("(k p) n -> p k n", p=P))\
                .then_inc(small_in[0], 16)
            sp.dma_start(gb[:, :], gate_b.to_broadcast([P, 2 * H])).then_inc(small_in[1], 16)
            sp.dma_start(stack[:, :], conv_w.rearrange("j (c p) -> (j c) p", p=P)).then_inc(small_in[2], 16)
            sp.dma_start(p_raw, p.rearrange("(a t) c -> t a c", t=P)).then_inc(small_in[4], 16)
            sp.dma_start(keys_raw, keys.rearrange("a n c -> n a c")).then_inc(small_in[5], 16)

            def load(slot, n, src, quarter, col):
                sp.wait_ge(lo_ready, n * HALVES + HALVES)
                sp.sem_inc(passed_s, 1)
                sp.dma_start(raw[slot], src.rearrange("(k p) n -> p k n", p=P)
                             [:, quarter * KQ:(quarter + 1) * KQ, bass.ds(col, NB)]).then_inc(raw_in[slot], 16)

            def stream(src, at, blocks, block0, order=ORDER_IN):
                with sp.Fori(0, blocks) as i:
                    for j, quarter in enumerate(order):
                        load(j, i * RING + (block0 * RING + j), src, quarter, i * NB + at)

            stream(w_in, Q_AT, 8, 0)
            stream(w_in, B_AT, 6, 8)
            stream(w_out, 0, BLOCKS_OUT, OUT0, ORDER_OUT)
            sp.wait_ge(conv_v, 2)
            sp.dma_start(g_rows, g_ffn.to_broadcast([P, D])).then_inc(gain_in[1], 16)
            stream(wq, 0, BLOCKS_WQ, WQ0)
            for j in range(2):
                load(j, PLE0 * RING + j, w_gate, j, 0)
            sp.wait_ge(now_used, UNITS + 1)
            sp.dma_start(ple_rows, g_ple.to_broadcast([P, D])).then_inc(gain_in[2], 16)
            sp.wait_ge(v_used, G + TT * SLOTS)
            sp.dma_start(wp, w_proj.rearrange("(k p) n -> p k n", p=P)).then_inc(wp_in, 16)
            for j in range(2, RING):
                load(j, PLE0 * RING + j, w_gate, j, 0)
            sp.dma_start(g_rows, g_final.to_broadcast([P, D])).then_inc(final_in, 16)
            stream(w_gate, NB, BLOCKS_PLE - 1, PLE0 + 1)
            for t in range(TT):
                for n, half in enumerate((slice(0, D // 2), slice(D // 2, D))):
                    sp.wait_ge(out_ready, 2 * t + n + 1)
                    sp.dma_start(out[t * P:(t + 1) * P, half], xn[:, t, half]).then_inc(stored[t], 16)
            for t in range(TT):
                sp.wait_ge(stored[t], 2 * 16)

        @block.gpsimd
        def _(pool):
            step = Count(pool, pool_c)
            step.done(pool.memset(ident[:, :], 0.0))
            step.done(pool.memset(ones[:, :], 1.0))
            step.done(pool.memset(mask[:, :], 0.0))
            step.done(pool.memset(eps[:, :], EPS))
            step.done(pool.memset(vS[:, :, :, HD:HW], 1.0))
            step.done(pool.memset(expert[:, TT * SLOTS:TT * SLOTS + 2 * G], 0))
            step.wait()
            pool.affine_select(out=ident[:, :], in_=ident[:, :], compare_op=ALU.not_equal, fill=1.0,
                               base=0, pattern=[[-1, P]], channel_multiplier=1).then_inc(consts, 1)
            pool.affine_select(out=tri, in_=ones[:, :], compare_op=ALU.is_ge, fill=0.0,
                               base=0, pattern=[[1, P]], channel_multiplier=-1).then_inc(consts, 1)
            pool.affine_select(out=mask[:, :], in_=mask[:, :], compare_op=ALU.is_ge, fill=FAR,
                               base=0, pattern=[[-1, P]], channel_multiplier=1).then_inc(consts, 1)
            pool.affine_select(out=last_row, in_=ones[:, :], compare_op=ALU.is_ge, fill=0.0,
                               base=-(P - 1), pattern=[[0, P]], channel_multiplier=1).then_inc(consts, 1)
            pool.iota(iota16[:, :], pattern=[[1, TOPK]], base=0, channel_multiplier=0,
                      allow_small_or_imprecise_dtypes=True).then_inc(consts, 1)

            def make_lo(n, slot):
                for part in range(HALVES):
                    buffer = (HALVES * slot + part) % SPLIT
                    pool.wait_ge(hi_ready, n * HALVES + (part + 1))
                    pool.tensor_tensor(w_lo[buffer][:, :, :], raw[slot][:, part * KH:(part + 1) * KH, :],
                                       w_hi[buffer][:, :, :].bitcast(F32), ALU.subtract).then_inc(lo_ready, 1)

            def gather_u(par, g):
                pool.wait_ge(idx_u_ready, g + 1)
                pool.wait_ge(u_used, g * G + G)
                pool.sem_inc(passed_p, 1)
                for s in range(G):
                    pool.indirect_dma_start(
                        out=u_rows[s], out_offset=None, in_=u_tab[:, :],
                        in_offset=bass.IndirectOffsetOnAxis(ap=idx_u[par][:, s:s + 1], axis=0),
                    ).then_inc(u_in[s], 16)

            def gather_v(par, g):
                pool.wait_ge(idx_v_ready, g + 1)
                for s in range(G):
                    pool.wait_ge(v_used, g * G + (s + 1))
                    pool.sem_inc(passed_p, 1)
                    pool.indirect_dma_start(
                        out=v_rows[s], out_offset=None, in_=v_tab[:, :],
                        in_offset=bass.IndirectOffsetOnAxis(ap=idx_v[par][:, s:s + 1], axis=0),
                    ).then_inc(v_in[s], 16)

            with pool.Fori(0, PLE0 - 1) as i:
                for j in range(RING):
                    make_lo(i * RING + j, j)
            gather_u(0, 0)
            for j in range(RING):
                make_lo((PLE0 - 1) * RING + j, j)
            gather_u(1, 1)
            pool.wait_ge(lo_ready, HALVES * RING * (PLE0 + 1))
            gather_v(0, 0)
            for j in range(2):
                make_lo(PLE0 * RING + j, j)
            with pool.Fori(1, TT * GROUPS // 2) as i:
                for par in range(2):
                    gather_u(par, i * 2 + par)
                    gather_v(1 - par, i * 2 + (par - 1))
            gather_v(1, TT * GROUPS - 1)

            for j in range(2, RING):
                make_lo(PLE0 * RING + j, j)
            with pool.Fori(PLE0 + 1, PLE0 + BLOCKS_PLE) as i:
                for j in range(RING):
                    make_lo(i * RING + j, j)

        @block.tensor
        def _(pe):
            pe.sem_inc(lo_ready, HALVES * RING)
            pe.sem_inc(half_used, SPLIT)
            pe.sem_inc(free_v, 4)
            pe.sem_inc(scores_out, 2)
            pe.sem_inc(sig_out, 4)
            pe.sem_inc(ple_used, 4)
            pe.sem_inc(u_used, G)
            pe.sem_inc(now_used, 1)
            pe.wait_ge(consts, 5)

            def transpose_norm(norm, tiles=(0, 1)):
                for t in tiles:
                    for q in range(4):
                        if q % 2 == 0:
                            pe.wait_ge(xn_ready, (norm * TT + t) * 2 + q // 2 + 1)
                        s = 4 * t + q
                        for j in range(4):
                            last = nc.tensor.transpose(ps[s][:, j * P:(j + 1) * P],
                                                       xn[:, t, (4 * q + j) * P:(4 * q + j + 1) * P], ident[:, :])
                        last.then_inc(tr_mm, 1)

            def wait_half(i, block0, half):
                pe.wait_ge(lo_ready, i * (HALVES * RING) + (HALVES * RING * (block0 + 1) + half + 1))

            def channel_block(b, i, block0, halves=(0, HALVES * RING)):
                for j in range(*halves):
                    wait_half(i, block0, j)
                    hi, lo = w_hi[j % SPLIT], w_lo[j % SPLIT]
                    for c in range(4):
                        out_c = ps[2 * b + c // 2][:, c % 2 * S:(c % 2 + 1) * S]
                        for k in range(KH):
                            kk = j * KH + k
                            nc.tensor.matmul(out_c, lo[:, k, c * P:(c + 1) * P], xT_hi[:, kk, :],
                                             start=(kk == 0 and c % 2 == 0), stop=False)
                            nc.tensor.matmul(out_c, hi[:, k, c * P:(c + 1) * P], xT_lo[:, kk, :],
                                             start=False, stop=False)
                            last = nc.tensor.matmul(out_c, hi[:, k, c * P:(c + 1) * P], xT_hi[:, kk, :],
                                                    start=False, stop=(kk == KT - 1 and c % 2 == 1))
                    last.then_inc(half_used, 1)

            def token_half(b, t, j, quarter):
                hi, lo = w_hi[j % SPLIT], w_lo[j % SPLIT]
                for k in range(KH):
                    kk = quarter * KQ + j % HALVES * KH + k
                    nc.tensor.matmul(ps[2 * b + t][:, :], xT_lo[:, kk, t * P:(t + 1) * P], hi[:, k, :],
                                     start=(j == 0 and k == 0), stop=False)
                    nc.tensor.matmul(ps[2 * b + t][:, :], xT_hi[:, kk, t * P:(t + 1) * P], lo[:, k, :],
                                     start=False, stop=False)
                    last = nc.tensor.matmul(ps[2 * b + t][:, :], xT_hi[:, kk, t * P:(t + 1) * P], hi[:, k, :],
                                            start=False, stop=(j == HALVES * RING - 1 and k == KH - 1))
                return last

            def token_block(b, i, block0, order=ORDER_IN, halves=HALVES * RING, tile0_has=0):
                for j in range(halves):
                    quarter = order[j // HALVES]
                    wait_half(i, block0, j)
                    if order == ORDER_OUT and j % HALVES == 0:
                        if quarter >= 2:
                            pe.wait_ge(yT_v, 2 * (quarter - 1))
                        else:
                            pe.wait_ge(conv_v, quarter + 1)
                    for t in range(1 if j < tile0_has else 0, TT):
                        last = token_half(b, t, j, quarter)
                    last.then_inc(half_used, 1)

            transpose_norm(0)
            pe.wait_ge(xT_v, 4)
            pe.wait_ge(small_in[2], 16)
            rows = TAPS * CT
            nc.tensor.transpose(ps[1][:, 0:rows], stack[:, :], ident[0:rows, 0:rows]).then_inc(setup_mm, 1)
            pe.wait_ge(small_in[4], 16)
            for t in range(TT):
                for k in range(PT):
                    last = nc.tensor.transpose(ps[2][:, k * S + t * P:k * S + (t + 1) * P],
                                               p_raw[:, t, k * P:(k + 1) * P], ident[:, :])
            last.then_inc(setup_mm, 1)

            def transpose_keys(n, bank):
                for j in range(4):
                    last = nc.tensor.transpose(ps[bank][:, j * P:(j + 1) * P], keys_raw[:, 4 * n + j, :], ident[:, :])
                last.then_inc(setup_mm, 1)

            pe.wait_ge(small_in[5], 16)
            transpose_keys(0, 3)
            pe.wait_ge(xT_v, 8)
            pe.wait_ge(gw_v, 1)
            for k in range(KT):
                both = gw_split[:, k, :, :].rearrange("p z n -> p (z n)")
                nc.tensor.matmul(ps[4][0:4 * H, 0:S], both, xT_lo[:, k, :], start=(k == 0), stop=False)
                last = nc.tensor.matmul(ps[4][0:4 * H, 0:S], both, xT_hi[:, k, :], start=False, stop=(k == KT - 1))
            last.then_inc(gT_mm, 1)
            for n in range(1, 4):
                transpose_keys(n, 4 + n)
            pe.wait_ge(gT_v, 1)
            for t in range(TT):
                last = nc.tensor.transpose(ps[4][:, S + t * 4 * H:S + (t + 1) * 4 * H], gT[:, t * P:(t + 1) * P],
                                           ident[0:4 * H, 0:4 * H])
            last.then_inc(gates_mm, 1)

            pe.wait_ge(setup_v, 3)
            with pe.Fori(0, 2) as i:
                for b in range(2):
                    pe.wait_ge(free_v, i * 4 + (2 * b + 2))
                    channel_block(b, i * 2, b)

            pe.wait_ge(lf_ready, 1)
            pe.wait_ge(setup_v, 6)
            nc.tensor.matmul(ps[4][:, 384:392], tri, lf[:, :, :].rearrange("p a h -> p (a h)"),
                             start=True, stop=True).then_inc(setup_mm, 1)
            pe.wait_ge(free_v, 4 + 8)
            for a in range(TT):
                for hh in range(H):
                    for d in range(2):
                        last = nc.tensor.matmul(
                            ps[6 + a][:, hh * P:(hh + 1) * P], qT[:, 2 * hh + d, a * P:(a + 1) * P],
                            kT[:, 2 * hh + d, a * P:(a + 1) * P], start=(hh == 0 and d == 0),
                            stop=(hh == H - 1 and d == 1))
            last.then_inc(mix_mm, 1)
            pe.wait_ge(diag_e_ready, 1)
            for a in range(TT):
                last = nc.tensor.matmul(ps[4 + a][:, :], ones[:, :],
                                        diag_e[:, a * H:(a + 1) * H, :].rearrange("p h s -> p (h s)"),
                                        start=True, stop=True)
            last.then_inc(mix_mm, 1)
            def tokens(first, last):
                with pe.Fori(first, last) as i:
                    for b in range(2):
                        pe.wait_ge(free_v, i * 4 + (2 * b + 10))
                        token_block(b, i * 2, 4 + b)

            tokens(0, 1)
            pe.wait_ge(mb_ready, 1)
            nc.tensor.matmul(ps[4][:, 0:2 * H], last_row, mb[:, :], start=True, stop=True).then_inc(mix_mm, 1)
            tokens(1, 2)

            pe.wait_ge(m_ready, 1)
            for c in range(CT):
                last = nc.tensor.transpose(ps[4 + c // 4][:, c % 4 * P:(c % 4 + 1) * P], kT[:, c, 0:P], ident[:, :])
            last.then_inc(mix_mm, 1)
            pe.wait_ge(sc_ready, 1)
            for c in range(TT * H):
                last = nc.tensor.transpose(ps[6 + c // H][:, c % H * P:(c % H + 1) * P], pw[:, c, :], ident[:, :])
            last.then_inc(mix_mm, 1)

            pe.wait_ge(scT_ready, 1)
            pe.wait_ge(free_v, 4 + 16)
            for hh in range(H):
                nc.tensor.matmul(ps[hh][:, 0:HW], scT[:, hh, :], vS[:, 0, hh, :], start=True, stop=True)\
                    .then_inc(bank_mm, 1)
            pe.wait_ge(kN_ready, 1)
            for n in range(2 * H):
                if n >= 4:
                    pe.wait_ge(bank_a, n - 3)
                nc.tensor.matmul(ps[(4 + n) % 8][:, 0:HW], kN[:, n // 2, n % 2 * P:(n % 2 + 1) * P],
                                 vS[:, 0, n // 2, :], start=True, stop=True).then_inc(bank_mm, 1)
            for hh in range(H):
                if hh % 2 == 0:
                    pe.wait_ge(bank_a, 4 + hh // 2 + 1)
                else:
                    pe.wait_ge(bank_v, hh // 2 + 1)
                nc.tensor.matmul(ps[4 + hh][:, 0:HW], scT[:, H + hh, :], vS[:, 1, hh, :], start=True, stop=True)\
                    .then_inc(bank_mm, 1)
            pe.wait_ge(bank_a, 8)
            pe.wait_ge(bank_v, 4)
            for hh in range(H):
                for d in range(2):
                    last = nc.tensor.matmul(ps[hh][:, 0:HW], qT[:, 2 * hh + d, P:2 * P], state[:, hh, d, :],
                                            start=(d == 0), stop=(d == 1))
                last.then_inc(bank_mm, 1)

            pe.wait_ge(bank_v, 8)
            def rounds(first, last):
                with pe.Fori(first, last) as i:
                    for b in range(2):
                        pe.wait_ge(free_v, i * 4 + (2 * b + 18))
                        channel_block(b, i * 2, 8 + b)

            rounds(0, 2)
            pe.wait_ge(y_ready, 1)
            for s in Y_STEPS:
                for j in range(4):
                    c = s % 2 * 4 + j
                    last = nc.tensor.transpose(ps[4 + s][:, j * P:(j + 1) * P],
                                               o_sig[:, s // 2, c * P:(c + 1) * P], ident[:, :])
                last.then_inc(yT_mm, 1)
            rounds(2, 3)

            with pe.Fori(0, 2) as i:
                for b in range(2):
                    pe.wait_ge(free_v, i * 4 + (2 * b + 30))
                    token_block(b, i * 2, OUT0 + b, ORDER_OUT)

            transpose_norm(1)
            pe.wait_ge(xT_v, 2 * 8)

            def scores(m):
                b = m % 2
                pe.wait_ge(q_out, 2 * (m + 1))
                pe.wait_ge(scores_out, m + 1)
                for t in range(TT):
                    for c in range(4):
                        last = nc.tensor.matmul(
                            ps[4 + 2 * b + t][:, c * P:(c + 1) * P], q_heads[b][:, c, t * P:(t + 1) * P],
                            keysT[:, 4 * m + c, :], start=(c == 0), stop=(c == 3))
                last.then_inc(scores_mm, 1)

            for m in range(BLOCKS_WQ):
                channel_block(m % 2, 0, WQ0 + m, (0, HALVES))
                if m:
                    scores(m - 1)
                channel_block(m % 2, 0, WQ0 + m, (HALVES, HALVES * RING))
            scores(BLOCKS_WQ - 1)
            pe.wait_ge(scores_mm, BLOCKS_WQ)
            pe.sem_inc(v_used, G)

            def add_rows(t, first, last):
                with pe.Fori(first, last) as i:
                    for par in range(2):
                        g = i * 2 + par
                        for s in range(G):
                            pe.wait_ge(v_in[s], g * 16 + 16)
                            pe.wait_ge(diag_ready, g * G + (s + 1))
                            for n in range(4):
                                last_mm = nc.tensor.matmul(ps[4 * t + n][:, :], v_diag[s],
                                                           v_rows[s][:, n * NB:(n + 1) * NB],
                                                           start=False, stop=True, skip_group_check=True)
                            last_mm.then_inc(v_used, 1)

            pe.wait_ge(scores_out, 6)
            for t in range(TT):
                for n in range(4):
                    nc.tensor.matmul(ps[4 * t + n][:, :], ident[:, :], h[:, t, n * NB:(n + 1) * NB],
                                     start=True, stop=True)
                if t == 0:
                    add_rows(0, 0, GROUPS // 2)
                else:
                    add_rows(1, GROUPS // 2, GROUPS // 2 + 1)
                    transpose_norm(2, (0,))
                    add_rows(1, GROUPS // 2 + 1, GROUPS // 2 + 2)
                    pe.wait_ge(xT_v, 2 * 8 + 4)
                    for j in range(SPLIT):
                        wait_half(0, PLE0, j)
                        token_half(0, 0, j, j // HALVES)
                    add_rows(1, GROUPS // 2 + 2, GROUPS)
            transpose_norm(2, (1,))

            pe.wait_ge(xT_v, 3 * 8)
            for m in range(BLOCKS_PLE):
                b = m % 2
                pe.wait_ge(ple_used, 2 * (m + 1))
                pe.wait_ge(wp_in, 16)
                for t in range(TT):
                    for k in range(PT):
                        last = nc.tensor.matmul(ps[4 + 2 * b + t][:, :], pT[:, k, t * P:(t + 1) * P],
                                                wp[:, k, m * NB:(m + 1) * NB], start=(k == 0), stop=(k == PT - 1))
                last.then_inc(ple_mm, 1)
                pe.wait_ge(sig_out, 2 * (m + 1))
                if m < BLOCKS_PLE - 1:
                    token_block(b, 0, PLE0 + m, tile0_has=0 if m else SPLIT)
                else:
                    token_block(b, 0, PLE0 + m, halves=SPLIT)
                    for t in range(TT):
                        for j in range(SPLIT, HALVES * RING):
                            wait_half(0, PLE0 + m, j)
                            last = token_half(b, t, j, j // HALVES)
                        last.then_inc(gate_mm, 1)

        @block.scalar
        def _(act):
            step = Count(act, act_c)
            act.wait_ge(pool_c, 6)

            def load_table(function):
                if step.n:
                    step.wait()
                step.done(nc.scalar.activation(unused[:, :], eps[:, :], function, bias=eps[:, :]))

            def square(t):
                step.done(nc.scalar.activation(xn[:, t, :], h[:, t, :], ACT.Square, accum_out=sq_sum[:, t:t + 1]))
                step.wait()

            def square_part(t, n):
                part = slice(n * NB, (n + 1) * NB)
                nc.scalar.activation(xn[:, t, part], h[:, t, part], ACT.Square,
                                     accum_out=sq_part[:, t, n:n + 1]).then_inc(sq_parts, 1)

            def square_blocks(n):
                for t in range(TT):
                    square_part(t, n)

            def mean_root(t, norm):
                if norm:
                    act.wait_ge(sum_ready, (norm - 1) * TT + t + 1)
                nc.scalar.activation(root[:, t:t + 1], sq_sum[:, t:t + 1], ACT.Sqrt, bias=eps[:, :],
                                     scale=1.0 / D).then_inc(sq_done, 1)

            def transposes_hi(norm, steps=range(8)):
                for s in steps:
                    act.wait_ge(tr_mm, norm * 8 + s + 1)
                    nc.scalar.activation(xT_hi[:, s % 4 * 4:s % 4 * 4 + 4, s // 4 * P:(s // 4 + 1) * P],
                                         ps[s][:, :].rearrange("p (k t) -> p k t", k=4), ACT.Copy)\
                        .then_inc(xT_a, 1)

            def make_hi(turn, n, slot):
                act.wait_ge(raw_in[slot], turn * 16 + 16)
                for part in range(HALVES):
                    act.wait_ge(half_used, n * HALVES + (part + 1))
                    nc.scalar.activation(w_hi[(HALVES * slot + part) % SPLIT][:, :, :],
                                         raw[slot][:, part * KH:(part + 1) * KH, :], ACT.Copy).then_inc(hi_ready, 1)

            def hi_quarters(first, last):
                for n in range(first, last):
                    make_hi(n // RING, n, n % RING)

            def hi_blocks(first, last):
                with act.Fori(first, last) as i:
                    for j in range(RING):
                        make_hi(i, i * RING + j, j)

            load_table(ACT.Sqrt)
            for t in range(TT):
                act.wait_ge(x_in[t], 16)
                square(t)
                mean_root(t, 0)
            act.dma_start(o_gain, g_mlstm.to_broadcast([P, CONV])).then_inc(small_in[3], 16)
            act.wait_ge(small_in[0], 16)
            nc.scalar.activation(gw_split[:, :, 0, :], gw, ACT.Copy).then_inc(gw_a, 1)
            transposes_hi(0)
            hi_quarters(0, 2)

            act.wait_ge(abs_ready, 1)
            step.done(nc.scalar.activation(exp_f[:, :, :], abs_f[:, :, :], ACT.Exp, scale=-1.0))
            step.wait()
            nc.scalar.activation(log_f[:, :, :], exp_f[:, :, :], ACT.Ln, bias=1.0).then_inc(softplus, 1)

            hi_quarters(2, RING)
            hi_blocks(1, 6)
            hi_quarters(6 * RING, 6 * RING + 2)

            act.wait_ge(m_ready, 1)
            for a in range(TT):
                for hh in range(H):
                    nc.scalar.activation(pw[:, a * H + hh, :], pw[:, a * H + hh, :], ACT.Exp,
                                         bias=neg_m[:, a, hh:hh + 1])
            nc.scalar.activation(decay[:, :, :], decay[:, :, :], ACT.Exp)
            nc.scalar.activation(floor[:, :, :], neg_m[:, :, :], ACT.Exp).then_inc(pw_ready, 1)

            hi_quarters(6 * RING + 2, 7 * RING)
            hi_blocks(7, 8)
            hi_quarters(8 * RING, 8 * RING + 2)

            act.wait_ge(free_v, 4 + 16)
            nc.scalar.activation(o_sig, o_sig, ACT.Sigmoid).then_inc(o_out, 1)
            for hh in range(H):
                act.wait_ge(bank_mm, hh + 1)
                nc.scalar.activation(num[:, 0, hh, :], ps[hh][:, 0:HW], ACT.Copy).then_inc(bank_a, 1)
            for hh in range(H):
                act.wait_ge(bank_mm, 4 + 2 * hh + 1)
                nc.scalar.activation(state[:, hh, 0, :], ps[(4 + 2 * hh) % 8][:, 0:HW], ACT.Copy).then_inc(bank_a, 1)
            for hh in range(H):
                act.wait_ge(bank_mm, 12 + hh + 1)
                nc.scalar.activation(num[:, 1, hh, :], ps[4 + hh][:, 0:HW], ACT.Copy).then_inc(bank_a, 1)

            act.wait_ge(rden_ready, 1)
            for a in range(TT):
                for hh in range(H):
                    step.done(nc.scalar.activation(ps[4 + hh][:, 0:HD], num[:, a, hh, 0:HD], ACT.Square,
                                                   scale=rden[:, a, hh:hh + 1], accum_out=head_sq[:, a, hh:hh + 1]))
                step.wait()
            nc.scalar.activation(head_root[:, :, :], head_sq[:, :, :], ACT.Sqrt, bias=eps[:, :], scale=1.0 / HD)\
                .then_inc(head_rt, 1)

            hi_quarters(8 * RING + 2, 9 * RING)
            hi_blocks(9, 13)
            hi_quarters(13 * RING, 14 * RING)
            act.wait_ge(conv_ready, 1)
            nc.scalar.activation(xT_hi[:, 0:4, :], conv[:, 0:4, :], ACT.Copy).then_inc(conv_a, 1)
            hi_quarters(OUT0 * RING, OUT0 * RING + 1)
            act.wait_ge(half_used, through(OUT0 - 1))
            for n, s in enumerate(Y_STEPS):
                act.wait_ge(yT_mm, n + 1)
                c = CT + s % 2 * 4
                nc.scalar.activation(xT_hi[:, c:c + 4, s // 2 * P:(s // 2 + 1) * P],
                                     ps[4 + s][:, :].rearrange("p (k t) -> p k t", k=4), ACT.Copy).then_inc(yT_a, 1)
            hi_quarters(OUT0 * RING + 1, (OUT0 + 1) * RING)
            act.wait_ge(conv_ready, 2)
            nc.scalar.activation(xT_hi[:, 4:8, :], conv[:, 4:8, :], ACT.Copy).then_inc(conv_a, 1)
            for n in range(BLOCKS_OUT):
                at_n = (OUT0 + n) * RING + 2
                hi_quarters(at_n if n else at_n + 2, at_n + RING)
                act.wait_ge(free_v, 4 + 2 * (OUT0 + n + 1))
                square_blocks(n)
            for t in range(TT):
                mean_root(t, 1)
            transposes_hi(1)

            def queries(m):
                if m >= 2:
                    act.wait_ge(scores_mm, m - 1)
                act.wait_ge(half_used, through(WQ0 + m))
                for j in range(2):
                    nc.scalar.activation(q_heads[m % 2][:, 2 * j:2 * j + 2, :].rearrange("p c t -> p (c t)"),
                                         ps[2 * (m % 2) + j][:, :], ACT.Copy).then_inc(q_out, 1)

            def scores(m):
                act.wait_ge(scores_mm, m + 1)
                nc.scalar.activation((scores1[:, 4 * m - 8:4 * m - 4, :] if m >= 2 else scores0[:, m, :, :])
                                     .rearrange("p c n -> p (c n)"), ps[4 + 2 * (m % 2)][:, :], ACT.Copy)
                nc.scalar.activation(scores1[:, 4 * m + 8:4 * m + 12, :].rearrange("p c n -> p (c n)"),
                                     ps[5 + 2 * (m % 2)][:, :], ACT.Copy).then_inc(scores_out, 1)

            def gates_of(first, heads):
                act.wait_ge(below_ready, 2 if first else 1)
                nc.scalar.activation(gate[:, first * TOPK:(first + heads) * TOPK], below_top[:, 0:heads * TOPK],
                                     ACT.Exp).then_inc(gate_exp, 1)

            for m in range(BLOCKS_WQ):
                at_m = (WQ0 + m) * RING + 2
                hi_quarters(at_m + (1 if m else 0), at_m + RING)
                queries(m)
                if m < BLOCKS_WQ - 1:
                    hi_quarters(at_m + RING, at_m + RING + 1)
                scores(m)
                if m == 2:
                    gates_of(0, EARLY)

            def group(par, g):
                act.wait_ge(u_used, g * G + 2 * G)
                nc.scalar.activation(act_now[par][:, :], dots[par][:, :], ACT.Gelu).then_inc(act_ready, 1)

            def groups(first, last):
                with act.Fori(first, last) as i:
                    for par in range(2):
                        group(par, i * 2 + par)

            def sums_squared(t):
                for n in range(4):
                    act.wait_ge(peer_out, 4 * t + n + 1)
                    square_part(t, n)
                mean_root(t, 2)

            act.wait_ge(scores_out, 2 + BLOCKS_WQ)
            group(0, 0)
            group(1, 1)
            with act.Fori(0, UNITS // 2) as i:
                for par in range(2):
                    act.wait_ge(now_used, i * 2 + (par + 1))
                    nc.scalar.activation(scores_now[:, :, :], scores1[:, bass.ds(i * 4 + 2 * par, 2), :],
                                         ACT.Copy).then_inc(now_ready, 1)
                    group(par, i * 2 + (par + 2))
            gates_of(EARLY, UNITS)
            groups(1 + UNITS // 2, GROUPS // 2 + 1)
            sums_squared(0)
            groups(GROUPS // 2 + 1, GROUPS // 2 + 2)
            transposes_hi(2, range(4))
            groups(GROUPS // 2 + 2, GROUPS)
            load_table(ACT.Sqrt)
            sums_squared(1)
            transposes_hi(2, range(4, 8))

            def sigmoid(m, t):
                nc.scalar.activation(sig[m % 2][t], ps[2 * (m % 2) + t][:, :], ACT.Sigmoid).then_inc(sig_out, 1)

            q0 = PLE0 * RING
            hi_quarters(q0 + 2, q0 + RING + 2)
            for m in range(BLOCKS_PLE - 1):
                act.wait_ge(half_used, through(PLE0 + m))
                if m >= 2:
                    act.wait_ge(ple_added, 2 * (m - 1))
                for t in range(TT):
                    sigmoid(m, t)
                hi_quarters(q0 + RING * (m + 1) + 2, min(q0 + RING * (m + 2) + 2, q0 + RING * BLOCKS_PLE))
                act.wait_ge(ple_added, 2 * (m + 1))
                square_blocks(m)
            m = BLOCKS_PLE - 1
            for t in range(TT):
                act.wait_ge(gate_mm, t + 1)
                sigmoid(m, t)
                load_table(ACT.Sqrt)
                act.wait_ge(ple_added, 2 * m + t + 1)
                square_part(t, m)
                mean_root(t, 3)
                if t == 0:
                    load_table(ACT.Sigmoid)

        @block.vector
        def _(dve):
            step = Count(dve, dve_c)
            v = nc.vector

            def normalise(norm, tiles=(0, 1)):
                if norm:
                    for t in tiles:
                        if norm == 2:
                            dve.wait_ge(sq_parts, 2 * TT * 2 + 4 * (t + 1))
                        else:
                            dve.wait_ge(sq_parts, (norm - 1) * TT * 4 + 6 + t + 1)
                        v.tensor_reduce(sq_sum[:, t:t + 1], sq_part[:, t, :], axis=AX.X, op=ALU.add)\
                            .then_inc(sum_ready, 1)
                gain = ple_rows if norm == 2 else g_rows
                for t in tiles:
                    dve.wait_ge(sq_done, norm * TT + t + 1)
                    step.done(v.reciprocal(rstd[:, t:t + 1], root[:, t:t + 1]))
                    step.wait()
                    if t == 0:
                        dve.wait_ge(final_in if norm == 3 else gain_in[norm], 16)
                    for half in (slice(0, D // 2), slice(D // 2, D)):
                        v.scalar_tensor_tensor(out=xn[:, t, half], in0=h[:, t, half], scalar=rstd[:, t:t + 1],
                                               in1=gain[:, half], op0=ALU.mult, op1=ALU.mult)\
                            .then_inc(out_ready if norm == 3 else xn_ready, 1)

            def transposes_lo(norm, steps=range(8)):
                for s in steps:
                    dve.wait_ge(xT_a, norm * 8 + s + 1)
                    to = slice(s % 4 * 4, s % 4 * 4 + 4), slice(s // 4 * P, (s // 4 + 1) * P)
                    v.tensor_tensor(xT_lo[:, to[0], to[1]], ps[s][:, :].rearrange("p (k t) -> p k t", k=4),
                                    xT_hi[:, to[0], to[1]].bitcast(F32), ALU.subtract).then_inc(xT_v, 1)

            def empty_channels(dst, n, scale=None):
                b = n % 2
                dve.wait_ge(half_used, through(n))
                for j in range(2):
                    to = dst[:, 4 * b + 2 * j:4 * b + 2 * j + 2, :].rearrange("p c t -> p (c t)")
                    if scale is None:
                        v.tensor_copy(to, ps[2 * b + j][:, :]).then_inc(free_v, 1)
                    else:
                        v.tensor_scalar(to, ps[2 * b + j][:, :], scale, None, ALU.mult).then_inc(free_v, 1)

            normalise(0)
            dve.wait_ge(gw_a, 1)
            v.tensor_tensor(gw_split[:, :, 1, :], gw, gw_split[:, :, 0, :].bitcast(F32), ALU.subtract)\
                .then_inc(gw_v, 1)
            transposes_lo(0)

            dve.wait_ge(setup_mm, 1)
            v.tensor_copy(cols[:, :, :].rearrange("p j c -> p (j c)"), ps[1][:, 0:TAPS * CT]).then_inc(setup_v, 1)
            dve.wait_ge(setup_mm, 2)
            v.tensor_copy(pT[:, :, :].rearrange("p k t -> p (k t)"), ps[2][:, :]).then_inc(setup_v, 1)
            for n, bank in enumerate((3, 5, 6, 7)):
                if n == 1:
                    dve.wait_ge(gT_mm, 1)
                    v.tensor_copy(gT, ps[4][0:4 * H, 0:S]).then_inc(gT_v, 1)
                dve.wait_ge(setup_mm, 3 + n)
                v.tensor_copy(keysT[:, 4 * n:4 * n + 4, :].rearrange("p a n -> p (a n)"), ps[bank][:, :])\
                    .then_inc(setup_v, 1)
            dve.wait_ge(small_in[1], 16)
            dve.wait_ge(gates_mm, 1)
            g_parts = ps[4][:, S:S + TT * 4 * H].rearrange("p (a z n) -> p a z n", a=TT, z=2)
            step.done(v.tensor_tensor(gates[:, :, :], g_parts[:, :, 0, :],
                                      gb[:, :].unsqueeze(1).to_broadcast([P, TT, 2 * H]), ALU.add))
            step.wait()
            step.done(v.tensor_tensor(gates[:, :, :], g_parts[:, :, 1, :], gates[:, :, :], ALU.add))
            step.wait()
            v.scalar_tensor_tensor(out=abs_f[:, :, :], in0=gates[:, :, H:2 * H], scalar=-1.0, in1=gates[:, :, H:2 * H],
                                   op0=ALU.mult, op1=ALU.max).then_inc(abs_ready, 1)
            dve.wait_ge(softplus, 1)
            v.scalar_tensor_tensor(out=lf[:, :, :], in0=gates[:, :, H:2 * H], scalar=0.0, in1=log_f[:, :, :],
                                   op0=ALU.min, op1=ALU.subtract).then_inc(lf_ready, 1)
            for n in range(2):
                empty_channels(qT, n)
            for n in range(2, 4):
                empty_channels(kT, n, scale=HD ** -0.5)
            dve.wait_ge(setup_mm, 7)
            step.done(v.tensor_copy(bcum[:, :, :].rearrange("p a h -> p (a h)"), ps[4][:, 384:392]))
            step.wait()
            step.done(v.tensor_tensor(e_in[:, :, :], gates[:, :, 0:H], bcum[:, :, :], ALU.subtract))
            step.wait()
            for a in range(TT):
                for hh in range(H):
                    last = v.tensor_scalar(diag_e[:, a * H + hh, :], ident[:, :], e_in[:, a, hh:hh + 1], None, ALU.mult)
            last.then_inc(diag_e_ready, 1)


            dve.wait_ge(mix_mm, 2)
            for a in range(TT):
                for hh in range(H):
                    step.done(v.scalar_tensor_tensor(
                        out=pw[:, a * H + hh, :], in0=ps[4 + a][:, hh * P:(hh + 1) * P],
                        scalar=bcum[:, a, hh:hh + 1], in1=mask[:, :], op0=ALU.add, op1=ALU.add))
            step.wait()
            step.done(v.tensor_reduce(m_in[:, :, :].rearrange("p a h -> p (a h)"), pw, axis=AX.X, op=ALU.max))
            step.wait()
            step.done(v.tensor_tensor(m_t[:, 0, :], bcum[:, 0, :], m_in[:, 0, :], ALU.max))
            step.done(v.tensor_tensor(mb[:, 0:H], bcum[:, 0, :], m_in[:, 0, :], ALU.max))
            v.tensor_copy(mb[:, H:2 * H], bcum[:, 0, :]).then_inc(mb_ready, 1)
            for n in range(4, 6):
                dve.wait_ge(half_used, through(n))
                for t in range(TT):
                    v.tensor_copy(vS[:, t, 2 * (n % 2):2 * (n % 2) + 2, 0:HD],
                                  ps[2 * (n % 2) + t][:, :].rearrange("p (h e) -> p h e", h=2)).then_inc(free_v, 1)
            dve.wait_ge(mix_mm, 3)
            step.done(v.tensor_copy(mb_last[:, :], ps[4][:, 0:2 * H]))
            step.wait()
            step.done(v.tensor_tensor(inter[:, :], bcum[:, 1, :], mb_last[:, 0:H], ALU.add))
            step.done(v.tensor_tensor(decay[:, 0, :], mb_last[:, H:2 * H], mb_last[:, 0:H], ALU.subtract))
            step.wait()
            step.done(v.tensor_tensor(m_t[:, 1, :], inter[:, :], m_in[:, 1, :], ALU.max))
            step.done(v.tensor_tensor(decay[:, 0, :], decay[:, 0, :], e_in[:, 0, :], ALU.add))
            step.wait()
            step.done(v.tensor_scalar(neg_m[:, :, :], m_t[:, :, :], -1.0, None, ALU.mult))
            v.tensor_tensor(decay[:, 1, :], inter[:, :], m_t[:, 1, :], ALU.subtract).then_inc(m_ready, 1)
            dve.wait_ge(pw_ready, 1)
            dve.wait_ge(mix_mm, 2)
            for a in range(TT):
                last = v.tensor_tensor(pw[:, a * H:(a + 1) * H, :], ps[6 + a][:, :].rearrange("p (h s) -> p h s", h=H),
                                       pw[:, a * H:(a + 1) * H, :], ALU.mult)
            last.then_inc(sc_ready, 1)
            for n in range(6, 8):
                dve.wait_ge(half_used, through(n))
                for t in range(TT):
                    v.tensor_copy(o_sig[:, t, n % 2 * NB:(n % 2 + 1) * NB], ps[2 * (n % 2) + t][:, :])\
                        .then_inc(free_v, 1)

            dve.wait_ge(mix_mm, 5)
            for a in range(TT):
                last = v.tensor_copy(scT[:, a * H:(a + 1) * H, :].rearrange("p h t -> p (h t)"), ps[6 + a][:, :])
            last.then_inc(scT_ready, 1)
            for hh in range(H):
                last = v.tensor_scalar(kN[:, hh, :], ps[4 + hh // 2][:, hh % 2 * HD:(hh % 2 + 1) * HD],
                                       decay[:, 0, hh:hh + 1], None, ALU.mult)
            last.then_inc(kN_ready, 1)
            for hh in range(H):
                dve.wait_ge(bank_mm, 4 + 2 * hh + 2)
                v.tensor_copy(state[:, hh, 1, :], ps[(5 + 2 * hh) % 8][:, 0:HW]).then_inc(bank_v, 1)
            dve.wait_ge(bank_a, 12)
            for hh in range(H):
                dve.wait_ge(bank_mm, 16 + hh + 1)
                v.scalar_tensor_tensor(out=num[:, 1, hh, :], in0=ps[hh][:, 0:HW], scalar=decay[:, 1, hh:hh + 1],
                                       in1=num[:, 1, hh, :], op0=ALU.mult, op1=ALU.add).then_inc(bank_v, 1)
            dve.wait_ge(bank_v, 8)
            step.done(v.scalar_tensor_tensor(out=den[:, :, :], in0=num[:, :, :, HD], scalar=-1.0,
                                             in1=num[:, :, :, HD], op0=ALU.mult, op1=ALU.max))
            step.wait()
            step.done(v.tensor_tensor(den[:, :, :], den[:, :, :], floor[:, :, :], ALU.max))
            step.wait()
            v.reciprocal(rden[:, :, :], den[:, :, :]).then_inc(rden_ready, 1)
            dve.wait_ge(o_out, 1)
            dve.wait_ge(small_in[3], 16)
            step.done(v.tensor_tensor(o_sig, o_sig, o_gain.unsqueeze(1).to_broadcast([P, TT, CONV]), ALU.mult))
            dve.wait_ge(head_rt, 1)
            step.done(v.reciprocal(head_scale[:, :, :], head_root[:, :, :]))
            step.wait()
            step.done(v.tensor_tensor(head_scale[:, :, :], head_scale[:, :, :], rden[:, :, :], ALU.mult))
            step.wait()
            for a in range(TT):
                for hh in range(H):
                    last = v.scalar_tensor_tensor(
                        out=o_sig[:, a, hh * HD:(hh + 1) * HD], in0=num[:, a, hh, 0:HD],
                        scalar=head_scale[:, a, hh:hh + 1], in1=o_sig[:, a, hh * HD:(hh + 1) * HD],
                        op0=ALU.mult, op1=ALU.mult)
            last.then_inc(y_ready, 1)
            dve.wait_ge(y_ready, 1)

            for n in range(8, 10):
                empty_channels(bT, n)
            for n in range(10, 12):
                empty_channels(zT, n)
            dve.wait_ge(free_v, 4 + 24)
            for n in range(12, 14):
                b = n % 2
                dve.wait_ge(half_used, through(n))
                if b == 1:
                    for m, s in enumerate(Y_STEPS):
                        dve.wait_ge(yT_a, m + 1)
                        c, to = CT + s % 2 * 4, slice(s // 2 * P, (s // 2 + 1) * P)
                        v.tensor_tensor(xT_lo[:, c:c + 4, to], ps[4 + s][:, :].rearrange("p (k t) -> p k t", k=4),
                                        xT_hi[:, c:c + 4, to].bitcast(F32), ALU.subtract).then_inc(yT_v, 1)
                for j in range(2):
                    zz = zT[:, 4 * b + 2 * j:4 * b + 2 * j + 2, :].rearrange("p c t -> p (c t)")
                    v.tensor_tensor(zz, ps[2 * b + j][:, :], zz, ALU.mult).then_inc(free_v, 1)
                dve.wait_ge(free_v, 4 + 2 * (n + 1))
                mine = range(4 * b, 4 * b + 4)
                for c in mine:
                    step.done(v.tensor_scalar(conv[:, c, :], zT[:, c, :], cols[:, 2, c:c + 1], None, ALU.mult))
                step.wait()
                for back in (1, 2):
                    for c in mine:
                        step.done(v.scalar_tensor_tensor(
                            out=conv[:, c, back:S], in0=zT[:, c, 0:S - back], scalar=cols[:, 2 - back, c:c + 1],
                            in1=conv[:, c, back:S], op0=ALU.mult, op1=ALU.add))
                    step.wait()
                four = slice(4 * b, 4 * b + 4)
                v.tensor_tensor(conv[:, four, :], conv[:, four, :], bT[:, four, :], ALU.mult).then_inc(conv_ready, 1)
                if b == 0:
                    dve.wait_ge(conv_a, 1)
                    v.tensor_tensor(xT_lo[:, four, :], conv[:, four, :], xT_hi[:, four, :].bitcast(F32),
                                    ALU.subtract).then_inc(conv_v, 1)
            dve.wait_ge(conv_a, 2)
            v.tensor_tensor(xT_lo[:, 4:8, :], conv[:, 4:8, :], xT_hi[:, 4:8, :].bitcast(F32), ALU.subtract)\
                .then_inc(conv_v, 1)

            for n in range(BLOCKS_OUT):
                b = n % 2
                dve.wait_ge(half_used, through(OUT0 + n))
                for t in range(TT):
                    hh = h[:, t, n * NB:(n + 1) * NB]
                    v.tensor_tensor(hh, ps[2 * b + t][:, :], hh, ALU.add).then_inc(free_v, 1)

            normalise(1)
            transposes_lo(1)

            def top16(lists):
                for part in (slice(0, 8), slice(8, 16)):
                    for s, _, src in lists:
                        step.done(v.max(s[:, part], src))
                    step.wait_apart(passed_v)
                    for s, n, src in lists:
                        step.done(v.max_index(n[:, part], s[:, part], src))
                    step.wait_apart(passed_v)
                    if part.start == 0:
                        for s, _, src in lists:
                            step.done(v.match_replace(src, s[:, part], src, FAR))
                        step.wait_apart(passed_v)

            def top_experts(heads, source, cand, hot, to):
                n = heads
                top16([(top_s[:, a, e, :], top_i[:, a, e, :], source(a, e)) for a in range(n) for e in range(2)])
                wide = [P, n, TOPK, TOPK]
                step.done(v.tensor_copy(top_f[:, 0:n, :, :].rearrange("p h e k -> p (h e k)"),
                                        top_i[:, 0:n, :, :].rearrange("p h e k -> p (h e k)")))
                step.done(v.tensor_tensor(cand.rearrange("p h (a b) -> p h a b", a=TOPK),
                                          top_s[:, 0:n, 0, :].unsqueeze(3).to_broadcast(wide),
                                          top_s[:, 0:n, 1, :].unsqueeze(2).to_broadcast(wide), ALU.add))
                step.wait_apart(passed_v)
                top16([(best[:, a, :], pos[:, a, :], cand[:, a, :]) for a in range(n)])
                step.done(v.tensor_scalar(pos_a[:, 0:n, :], pos[:, 0:n, :], 4, None, ALU.logical_shift_right))
                step.done(v.tensor_scalar(pos_b[:, 0:n, :], pos[:, 0:n, :], TOPK - 1, None, ALU.bitwise_and))
                step.done(v.tensor_copy(gate[:, bass.ds(to, n * TOPK)],
                                        best[:, 0:n, :].rearrange("p h k -> p (h k)")))
                step.wait()
                step.done(v.tensor_copy(pos_f[0][:, 0:n, :], pos_a[:, 0:n, :]))
                step.done(v.tensor_copy(pos_f[1][:, 0:n, :], pos_b[:, 0:n, :]))
                step.wait()
                for e in range(2):
                    step.done(v.tensor_tensor(hot, pos_f[e][:, 0:n, :].unsqueeze(3).to_broadcast(wide),
                                              iota16[:, :].unsqueeze(1).unsqueeze(1).to_broadcast(wide),
                                              ALU.is_equal))
                    step.wait()
                    step.done(v.tensor_tensor(hot, hot, top_f[:, 0:n, e, :].unsqueeze(2).to_broadcast(wide), ALU.mult))
                    step.wait()
                    step.done(v.tensor_reduce(sel[e][:, 0:n, :], hot, axis=AX.X, op=ALU.add))
                    step.wait()
                step.done(v.scalar_tensor_tensor(out=expert[:, bass.ds(to, n * TOPK)],
                                                 in0=sel[0][:, 0:n, :].rearrange("p h k -> p (h k)"), scalar=float(NK),
                                                 in1=sel[1][:, 0:n, :].rearrange("p h k -> p (h k)"),
                                                 op0=ALU.mult, op1=ALU.add))
                step.wait_apart(passed_v)

            def below_largest(first, heads):
                per_head = gate[:, first * TOPK:(first + heads) * TOPK].rearrange("p (n k) -> p n k", k=TOPK)
                v.tensor_tensor(below_top[:, 0:heads * TOPK].rearrange("p (n k) -> p n k", k=TOPK), per_head,
                                per_head[:, :, 0:1].to_broadcast([P, heads, TOPK]), ALU.subtract)\
                    .then_inc(below_ready, 1)

            def over_sum(first, heads):
                per_head = gate[:, first * TOPK:(first + heads) * TOPK].rearrange("p (n k) -> p n k", k=TOPK)
                sums, inv = gate_sum[:, first:first + heads], gate_inv[:, first:first + heads]
                dve.wait_ge(gate_exp, 2 if first else 1)
                step.done(v.tensor_reduce(sums, per_head, axis=AX.X, op=ALU.add))
                step.wait()
                step.done(v.reciprocal(inv, sums))
                step.wait()
                step.done(v.tensor_tensor(per_head, per_head, inv.unsqueeze(2).to_broadcast([P, heads, TOPK]),
                                          ALU.mult))
                step.wait()

            dve.wait_ge(consts, 5)
            dve.wait_ge(pool_c, 6)
            for m in range(EARLY // 2):
                dve.wait_ge(scores_out, 2 + (m + 1))
                dve.sem_inc(passed_v, 1)
                top_experts(2, lambda a, e: scores0[:, m, 2 * a + e, :],
                            tmp[:, 0:2 * CAND].rearrange("p (h c) -> p h c", h=2),
                            tmp[:, 2 * CAND:4 * CAND].rearrange("p (h k a) -> p h k a", h=2, k=TOPK),
                            2 * m * TOPK)
                v.tensor_copy(idx_u[m][:, :], expert[:, m * G:(m + 1) * G]).then_inc(idx_u_ready, 1)
            below_largest(0, EARLY)

            def dot_products(t, par, g):
                for s in range(G):
                    dve.wait_ge(u_in[s], g * 16 + 16)
                    v.tensor_tensor_reduce(out=u_rows[s], in0=u_rows[s], in1=xn[:, t, :], scale=1.0,
                                           scalar=0.0, op0=ALU.mult, op1=ALU.add,
                                           accum_out=dots[par][:, s:s + 1]).then_inc(u_used, 1)
                v.tensor_copy(idx_u[par][:, :], expert[:, bass.ds(g * G + 2 * G, G)]).then_inc(idx_u_ready, 1)

            def v_list(par, g):
                v.tensor_copy(idx_v[par][:, :], expert[:, bass.ds(g * G, G)]).then_inc(idx_v_ready, 1)

            def diagonals(par, g):
                v.tensor_copy(gate_now[par][:, :], gate[:, bass.ds(g * G, G)]).then_inc(gate_c, 1)
                dve.wait_ge(act_ready, g + 1)
                dve.wait_ge(gate_c, g + 1)
                for s in range(G):
                    dve.wait_ge(v_used, g * G + (s + 1))
                    v.tensor_scalar(v_diag[s], ident[:, :], act_now[par][:, s:s + 1],
                                    gate_now[par][:, s:s + 1], ALU.mult, ALU.mult).then_inc(diag_ready, 1)

            def groups(t, first, last):
                with dve.Fori(first, last) as i:
                    for par in range(2):
                        dot_products(t, par, i * 2 + par)
                        diagonals(1 - par, i * 2 + (par - 1))
                        v_list(par, i * 2 + par)

            def sum_and_normalise(t):
                dve.wait_ge(v_used, G + (t + 1) * SLOTS)
                for n in range(4):
                    v.tensor_copy(h[:, t, n * NB:(n + 1) * NB], ps[4 * t + n][:, :]).then_inc(peer_out, 1)
                dve.wait_ge(peer_out, 4 * (t + 1))
                normalise(2, (t,))

            dot_products(0, 0, 0)
            v_list(0, 0)
            over_sum(0, EARLY)
            dot_products(0, 1, 1)
            diagonals(0, 0)
            v_list(1, 1)
            base, first = step.n, step.steps
            with dve.Fori(0, UNITS // 2) as i:
                for par in range(2):
                    dot_products(0, par, i * 2 + (par + 2))
                    diagonals(1 - par, i * 2 + (par + 1))
                    v_list(par, i * 2 + (par + 2))
                    step.n = i * (2 * UNIT_STEPS) + (base + par * UNIT_STEPS)
                    dve.wait_ge(now_ready, i * 2 + (par + 1))
                    dve.sem_inc(passed_v, 1)
                    top_experts(1, lambda a, e: scores_now[:, e, :],
                                tmp[:, 512:512 + CAND].rearrange("p (h c) -> p h c", h=1),
                                tmp[:, 768:768 + CAND].rearrange("p (h k a) -> p h k a", h=1, k=TOPK),
                                i * (2 * TOPK) + (EARLY + par) * TOPK)
                    dve.sem_inc(now_used, 1)
            assert step.steps - first == 2 * UNIT_STEPS, step.steps - first
            step.n = base + UNITS * UNIT_STEPS
            below_largest(EARLY, UNITS)
            over_sum(EARLY, UNITS)
            groups(0, 1 + UNITS // 2, GROUPS // 2)
            groups(1, GROUPS // 2, GROUPS // 2 + 1)
            sum_and_normalise(0)
            groups(1, GROUPS // 2 + 1, GROUPS // 2 + 2)
            transposes_lo(2, range(4))
            groups(1, GROUPS // 2 + 2, GROUPS)
            diagonals(1, TT * GROUPS - 1)
            sum_and_normalise(1)
            transposes_lo(2, range(4, 8))
            for n in range(BLOCKS_PLE - 1):
                b = n % 2
                dve.wait_ge(ple_mm, n + 1)
                dve.wait_ge(sig_out, 4 + 2 * (n + 1))
                for t in range(TT):
                    v.tensor_tensor(sig[b][t], ps[4 + 2 * b + t][:, :], sig[b][t], ALU.mult).then_inc(ple_used, 1)
                dve.wait_ge(ple_used, 4 + 2 * (n + 1))
                for t in range(TT):
                    hh = h[:, t, n * NB:(n + 1) * NB]
                    v.tensor_tensor(hh, hh, sig[b][t], ALU.add).then_inc(ple_added, 1)
            n = BLOCKS_PLE - 1
            dve.wait_ge(ple_mm, n + 1)
            for t in range(TT):
                dve.wait_ge(sig_out, 4 + 2 * n + t + 1)
                v.tensor_tensor(sig[1][t], ps[6 + t][:, :], sig[1][t], ALU.mult).then_inc(ple_used, 1)
                dve.wait_ge(ple_used, 4 + 2 * n + t + 1)
                hh = h[:, t, n * NB:(n + 1) * NB]
                v.tensor_tensor(hh, hh, sig[1][t], ALU.add).then_inc(ple_added, 1)
                normalise(3, (t,))


_VIEWS = {
    "x": (S, D), "p": (S, PLE), "norm_mix_g": (1, D), "w_in": (D, GATES_AT + 2 * H), "conv_w": (TAPS, CONV),
    "mlstm_gate_b": (1, 2 * H), "mlstm_norm_g": (1, H * HD), "w_out": (D, D), "norm_ffn_g": (1, D),
    "peer_wq": (D, D), "peer_keys": (2 * PH, NK, P), "peer_u": (NK * NK, D), "peer_v": (NK * NK, D),
    "norm_ple_g": (1, D), "ple_w_gate": (D, D), "ple_w_proj": (PLE, D), "norm_final_g": (1, D),
}


def kernel(**inputs):
    import numpy as _np
    import concourse.bacc as _bacc
    from concourse import mybir as _mybir
    from concourse.bass_utils import run_bass_kernel_spmd as _run

    nc = _bacc.Bacc("TRN2", target_bir_lowering=False, num_devices=1)
    arrays, args = {}, []
    for name, shape in _VIEWS.items():
        a = _np.ascontiguousarray(inputs[name]).reshape(shape)
        arrays[f"in_{name}"] = a
        args.append(nc.dram_tensor(f"in_{name}", shape, _mybir.dt.from_np(a.dtype), kind="ExternalInput").ap())
    args.append(nc.dram_tensor("out_h", (S, D), F32, kind="ExternalOutput").ap())
    build(nc, *args)
    r = _run(nc, [arrays], core_ids=[0])
    return r.results[0]["out_h"].reshape(1, S, D)
```
